# Optimizing a Trainium2 kernel written in Bass

```python
import jax, jax.numpy as jnp
from jax import lax
import numpy as np

D_MODEL = 2048
BATCH = 1
SEQ = 256
DEPTH = 1

GLA_HEADS = 4
GLA_DK = D_MODEL // 2 // GLA_HEADS
GLA_DV = D_MODEL // GLA_HEADS
GLA_KEY_WIDTH = GLA_HEADS * GLA_DK
GLA_VAL_WIDTH = GLA_HEADS * GLA_DV
GLA_LOW_RANK = 16
GLA_TAU = 16.0
GLA_CHUNK = 64
GLA_NORM_EPS = 1e-5
LRU_WIDTH = D_MODEL
LRU_BLOCKS = 8
LRU_BLOCK = LRU_WIDTH // LRU_BLOCKS
LRU_C = 8.0
CONV_WIDTH = 4
D_FF = -(-8 * D_MODEL // (3 * 256)) * 256
N_BRANCHES = 2
DEEPNORM_ALPHA = (2 * DEPTH) ** 0.25
DEEPNORM_BETA = (8 * DEPTH) ** -0.25
LN_EPS = 1e-5

SPLIT_SIZES = (GLA_KEY_WIDTH, GLA_KEY_WIDTH, GLA_VAL_WIDTH, GLA_VAL_WIDTH, GLA_LOW_RANK,
               LRU_WIDTH, LRU_WIDTH, N_BRANCHES * D_MODEL)
SPLIT_POINTS = [sum(SPLIT_SIZES[:i + 1]) for i in range(len(SPLIT_SIZES) - 1)]
IN_COLS = sum(SPLIT_SIZES)

kernel_name = "hybrid_gla_rglru_deepnorm"

def layer_norm(x, g, b):
    xf = x.astype(jnp.float32)
    mu = jnp.mean(xf, axis=-1, keepdims=True)
    var = jnp.mean(jnp.square(xf - mu), axis=-1, keepdims=True)
    y = (xf - mu) * lax.rsqrt(var + LN_EPS)
    return (y * g + b).astype(x.dtype)

def rms_norm(x, g):
    xf = x.astype(jnp.float32)
    y = xf * lax.rsqrt(jnp.mean(jnp.square(xf), axis=-1, keepdims=True) + GLA_NORM_EPS)
    return (y * g).astype(x.dtype)

def gla_chunked(q, k, v, log_a):
    B, T, H, dk = q.shape
    dv = v.shape[-1]
    C = GLA_CHUNK
    N = T // C
    out_dtype = v.dtype

    def to_chunks(t):
        return t.reshape(B, N, C, H, t.shape[-1]).transpose(1, 0, 3, 2, 4).astype(jnp.float32)

    qc, kc, vc, gc = to_chunks(q), to_chunks(k), to_chunks(v), to_chunks(log_a)
    bcum = jnp.cumsum(gc, axis=3)
    b_last = bcum[:, :, :, -1:, :]
    q_dec = qc * jnp.exp(bcum)
    k_inv = kc * jnp.exp(-bcum)
    k_end = kc * jnp.exp(b_last - bcum)

    causal = jnp.tril(jnp.ones((C, C), dtype=bool))
    scores = jnp.einsum('nbhik,nbhjk->nbhij', q_dec, k_inv)
    scores = jnp.where(causal, scores, 0.0)
    o_intra = jnp.einsum('nbhij,nbhjv->nbhiv', scores, vc)

    def step(S, inp):
        q_d, k_e, v_c, b_l = inp
        o = jnp.einsum('bhik,bhkv->bhiv', q_d, S)
        S = S * jnp.exp(b_l)[:, :, 0, :, None] + jnp.einsum('bhjk,bhjv->bhkv', k_e, v_c)
        return S, o

    S0 = jnp.zeros((B, H, dk, dv), jnp.float32)
    _, o_inter = lax.scan(step, S0, (q_dec, k_end, vc, b_last))
    o = (o_intra + o_inter).transpose(1, 0, 3, 2, 4).reshape(B, T, H, dv)
    return o.astype(out_dtype)

def causal_depthwise_conv(x, w, b):
    K, W = w.shape
    y = lax.conv_general_dilated(x, w[:, None, :], window_strides=(1,), padding=[(K - 1, 0)],
                                 dimension_numbers=('NWC', 'WIO', 'NWC'), feature_group_count=W)
    return y + b

def rg_lru(x, w_a, b_a, w_x, b_x, lam):
    B, T, W = x.shape
    xb = x.reshape(B, T, LRU_BLOCKS, LRU_BLOCK)
    r = jax.nn.sigmoid(jnp.einsum('btni,nij->btnj', xb, w_a).reshape(B, T, W) + b_a)
    i = jax.nn.sigmoid(jnp.einsum('btni,nij->btnj', xb, w_x).reshape(B, T, W) + b_x)
    log_a = (-LRU_C * jax.nn.softplus(-lam.astype(jnp.float32))) * r.astype(jnp.float32)
    a = jnp.exp(log_a)
    u = jnp.sqrt(-jnp.expm1(2.0 * log_a)) * (i * x).astype(jnp.float32)

    def combine(left, right):
        a1, h1 = left
        a2, h2 = right
        return a1 * a2, a2 * h1 + h2

    _, h = lax.associative_scan(combine, (a, u), axis=1)
    return h.astype(x.dtype)

def hybrid_mixer(x, w_in, gla_w_alpha, gla_b_alpha, gla_norm_g, gla_w_o, conv_w, conv_b,
                 lru_w_a, lru_b_a, lru_w_x, lru_b_x, lru_lambda, rnn_w_o, w_out):
    B, T, _ = x.shape
    proj = jnp.einsum('btd,dc->btc', x, w_in)
    q, k, v, g_out, lr, rx, ry, gates = jnp.split(proj, SPLIT_POINTS, axis=-1)

    q = q.reshape(B, T, GLA_HEADS, GLA_DK) * (GLA_DK ** -0.5)
    k = k.reshape(B, T, GLA_HEADS, GLA_DK)
    v = v.reshape(B, T, GLA_HEADS, GLA_DV)
    alpha_pre = jnp.einsum('btr,rk->btk', lr, gla_w_alpha) + gla_b_alpha
    log_a = (jax.nn.log_sigmoid(alpha_pre.astype(jnp.float32)) / GLA_TAU).reshape(B, T, GLA_HEADS, GLA_DK)
    o = gla_chunked(q, k, v, log_a)
    o = rms_norm(o, gla_norm_g).reshape(B, T, GLA_VAL_WIDTH)
    y_a = jnp.einsum('btv,vd->btd', o * jax.nn.silu(g_out), gla_w_o)

    hx = causal_depthwise_conv(rx, conv_w, conv_b)
    hx = rg_lru(hx, lru_w_a, lru_b_a, lru_w_x, lru_b_x, lru_lambda)
    y_b = jnp.einsum('btw,wd->btd', hx * jax.nn.gelu(ry), rnn_w_o)

    g_a, g_b = jnp.split(jax.nn.sigmoid(gates), 2, axis=-1)
    merged = g_a * y_a + g_b * y_b
    return jnp.einsum('btd,de->bte', merged, w_out)

def swiglu_ffn(x, w_gate_up, w_down):
    h = jnp.einsum('btd,df->btf', x, w_gate_up)
    gate, up = jnp.split(h, 2, axis=-1)
    return jnp.einsum('btf,fd->btd', jax.nn.silu(gate) * up, w_down)

def setup_inputs(seed: int = 0) -> dict:
    key = jax.random.key(seed)
    ks = jax.random.split(key, 24)
    f32 = jnp.float32
    nrm = lambda k, shape, s: jax.random.normal(k, shape, f32) * s
    beta = DEEPNORM_BETA
    col_scale = jnp.concatenate([
        jnp.full((n,), s, f32) for n, s in zip(
            SPLIT_SIZES, (1.0, 1.0, beta, 1.0, 1.0, beta, 1.0, 1.0))])
    x = jax.random.normal(ks[0], (BATCH, SEQ, D_MODEL), f32)
    w_in = nrm(ks[1], (DEPTH, D_MODEL, IN_COLS), D_MODEL ** -0.5) * col_scale
    gla_w_alpha = nrm(ks[2], (DEPTH, GLA_LOW_RANK, GLA_KEY_WIDTH), GLA_LOW_RANK ** -0.5)
    gla_b_alpha = nrm(ks[3], (DEPTH, GLA_KEY_WIDTH), 0.1)
    gla_norm_g = 1.0 + nrm(ks[4], (DEPTH, GLA_DV), 0.02)
    gla_w_o = nrm(ks[5], (DEPTH, GLA_VAL_WIDTH, D_MODEL), GLA_VAL_WIDTH ** -0.5 * beta)
    conv_w = nrm(ks[6], (DEPTH, CONV_WIDTH, LRU_WIDTH), CONV_WIDTH ** -0.5)
    conv_b = nrm(ks[7], (DEPTH, LRU_WIDTH), 0.02)
    lru_w_a = nrm(ks[8], (DEPTH, LRU_BLOCKS, LRU_BLOCK, LRU_BLOCK), LRU_BLOCK ** -0.5)
    lru_b_a = nrm(ks[9], (DEPTH, LRU_WIDTH), 0.02)
    lru_w_x = nrm(ks[10], (DEPTH, LRU_BLOCKS, LRU_BLOCK, LRU_BLOCK), LRU_BLOCK ** -0.5)
    lru_b_x = nrm(ks[11], (DEPTH, LRU_WIDTH), 0.02)
    u = jax.random.uniform(ks[12], (DEPTH, LRU_WIDTH), f32, 0.9, 0.999)
    s = u ** (1.0 / LRU_C)
    lru_lambda = jnp.log(s) - jnp.log1p(-s)
    rnn_w_o = nrm(ks[13], (DEPTH, LRU_WIDTH, D_MODEL), LRU_WIDTH ** -0.5 * beta)
    w_out = nrm(ks[14], (DEPTH, D_MODEL, D_MODEL), D_MODEL ** -0.5 * beta)
    ln1_g = 1.0 + nrm(ks[15], (DEPTH, D_MODEL), 0.02)
    ln1_b = nrm(ks[16], (DEPTH, D_MODEL), 0.02)
    w_gate_up = nrm(ks[17], (DEPTH, D_MODEL, 2 * D_FF), D_MODEL ** -0.5)
    w_down = nrm(ks[18], (DEPTH, D_FF, D_MODEL), D_FF ** -0.5 * beta)
    ln2_g = 1.0 + nrm(ks[19], (DEPTH, D_MODEL), 0.02)
    ln2_b = nrm(ks[20], (DEPTH, D_MODEL), 0.02)
    return {"x": x, "w_in": w_in, "gla_w_alpha": gla_w_alpha, "gla_b_alpha": gla_b_alpha,
            "gla_norm_g": gla_norm_g, "gla_w_o": gla_w_o, "conv_w": conv_w, "conv_b": conv_b,
            "lru_w_a": lru_w_a, "lru_b_a": lru_b_a, "lru_w_x": lru_w_x, "lru_b_x": lru_b_x,
            "lru_lambda": lru_lambda, "rnn_w_o": rnn_w_o, "w_out": w_out,
            "ln1_g": ln1_g, "ln1_b": ln1_b, "w_gate_up": w_gate_up, "w_down": w_down,
            "ln2_g": ln2_g, "ln2_b": ln2_b}

def reference(x, w_in, gla_w_alpha, gla_b_alpha, gla_norm_g, gla_w_o, conv_w, conv_b,
              lru_w_a, lru_b_a, lru_w_x, lru_b_x, lru_lambda, rnn_w_o, w_out,
              ln1_g, ln1_b, w_gate_up, w_down, ln2_g, ln2_b):
    h = x
    for l in range(DEPTH):
        mix = hybrid_mixer(h, w_in[l], gla_w_alpha[l], gla_b_alpha[l], gla_norm_g[l], gla_w_o[l],
                           conv_w[l], conv_b[l], lru_w_a[l], lru_b_a[l], lru_w_x[l], lru_b_x[l],
                           lru_lambda[l], rnn_w_o[l], w_out[l])
        h = layer_norm(DEEPNORM_ALPHA * h + mix, ln1_g[l], ln1_b[l])
        h = layer_norm(DEEPNORM_ALPHA * h + swiglu_ffn(h, w_gate_up[l], w_down[l]), ln2_g[l], ln2_b[l])
    return h


_drawn_inputs = setup_inputs


def setup_inputs(seed=0):
    import zlib

    import numpy as np

    out = dict(_drawn_inputs(seed))
    spreads = {}
    factors = {'gla_w_alpha': 5.452,
     'gla_b_alpha': 8.0,
     'gla_norm_g': 36.322,
     'conv_b': 52.4,
     'lru_w_a': 64.0,
     'lru_b_a': 64.0,
     'lru_w_x': 46.432,
     'lru_b_x': 64.0,
     'lru_lambda': 46.264,
     'ln1_b': 2.788,
     'ln2_g': 8.522,
     'ln2_b': 8.375,
     'conv_w': 8.0,
     'rnn_w_o': 8.0}
    for name, (base, spread) in spreads.items():
        noise = np.random.default_rng([zlib.crc32(name.encode()), seed]).standard_normal(out[name].shape)
        drawn = base * np.exp(spread * noise) if base else spread * noise
        out[name] = __import__('jax').numpy.asarray(drawn.astype(out[name].dtype))
    for name, factor in factors.items():
        out[name] = (out[name] * factor).astype(out[name].dtype)
    return out
```

```python
from contextlib import ExitStack

import numpy as np

import concourse.bass as bass
from concourse import mybir

F32 = mybir.dt.float32
F32R = mybir.dt.float32r
BF16 = mybir.dt.bfloat16
ALU = mybir.AluOpType
ACT = mybir.ActivationFunctionType

P = 128
D = 2048
T = 256
TT = T // P
KT = D // P
HEADS = 4
DK = 256
DV = 512
CHUNK = 64
NCHUNK = T // CHUNK
RANK = 16
TAU = 16.0
LRU_C = 8.0
CONV = 4
FF = 5632
ALPHA = 2 ** 0.25
EPS = 1e-5
LN_DVE = 1280

COL_Q, COL_K, COL_V, COL_G = 0, 1024, 2048, 4096
COL_LR = 6144
COL_RX = COL_LR + RANK
COL_RY = COL_RX + D
COL_GA = COL_RY + D
COL_GB = COL_GA + D

PIECE = 1024
RING = 4
SLOTS = 8
GROUP = 256
N_RX, N_LG, N_HEAD, N_B, N_A, N_OUT, N_FFN, N_DOWN = 4, 1, 16, 8, 8, 4, FF // GROUP, FF // P // 4
I_RX = 0
I_LG = I_RX + N_RX
I_HEAD = I_LG + N_LG
I_B = I_HEAD + N_HEAD
I_A = I_B + N_B
I_OUT = I_A + N_A
I_FFN = I_OUT + N_OUT
I_DOWN = I_FFN + N_FFN
ITERS = I_DOWN + N_DOWN
G_RX = 0
G_HEAD = G_RX + 2 * N_RX
G_B = G_HEAD + 6 * HEADS
G_A = G_B + 2 * N_B
G_FFN = G_A + 2 * N_A
G_END = G_FFN + 2 * N_FFN

PAR = {}
_at = 0
for _name, _n in (("conv_w", CONV * KT), ("conv_b", KT), ("b_a", KT), ("b_x", KT), ("lambda", KT),
                  ("b_alpha", HEADS * DK // P), ("norm_g", DV // P), ("ln1_g", KT), ("ln1_b", KT)):
    PAR[_name] = _at
    _at += _n
N_PAR = _at

FREE = 1

LOG1P_TERMS = 9


class Steps:

    def __init__(self, eng, sem, trip=0, per=0):
        self.eng, self.sem, self.base, self.n, self.per = eng, sem, trip * per, 0, per

    def step(self, instruction):
        instruction.then_inc(self.sem, 1)
        self.n += 1

    def wait(self):
        self.eng.wait_ge(self.sem, self.base + self.n)

    def end(self):
        assert self.n == self.per, (self.n, self.per)


def build(nc, x, w_in, w_alpha, w_o, lru_w, rnn_o, w_out, w_gu, w_down, params, ln1_g, ln1_b, ln2_g, ln2_b, out):
    with ExitStack() as ctx:
        def sb(name, shape, dt=F32, stack=ctx):
            return stack.enter_context(nc.sbuf_tensor(name, shape, dt))

        def sem(name):
            return ctx.enter_context(nc.semaphore(name))

        raw = sb("raw", [P, RING, PIECE])
        w_hi = sb("w_hi", [P, RING, PIECE], F32R)
        w_lo = sb("w_lo", [P, RING, PIECE], F32R)
        x_t = sb("x_t", [P, KT, 2 * T], F32R)
        par = sb("par", [P, N_PAR])
        ident = sb("ident", [P, P])
        corr = sb("corr", [P, 4, T])
        one_col = sb("one_col", [P, 1])
        scratch = sb("scratch", [P, 2])
        gsum = sb("gsum", [P, 2, T])
        psum = ctx.enter_context(nc.psum_tensor("psum", [P, 8, 2 * T], F32))

        with ExitStack() as st:
            lr_raw = sb("lr_raw", [P, KT, P], stack=st)
            lr_hi = sb("lr_hi", [P, KT, P], F32R, stack=st)
            lr_lo = sb("lr_lo", [P, KT, P], F32R, stack=st)
            x_in = sb("x_in", [P, TT, D], stack=st)
        with ExitStack() as st:
            gates = sb("gates", [P, KT, 2 * T], stack=st)
        with ExitStack() as st:
            h_ff = sb("h_ff", [P, FF // P, T], stack=st)
            tok_g1 = sb("tok_g1", [P, D], stack=st)
            tok_b1 = sb("tok_b1", [P, D], stack=st)
        o_t = sb("o_t", [P, KT, 2 * T], F32R)
        b_t = sb("b_t", [P, KT, 2 * T], F32R)
        with ExitStack() as st:
            merged = sb("merged", [P, KT, T], stack=st)
            yb = sb("yb", [P, 2, T], stack=st)
            stage = sb("stage", [P, 4, 2 * T], F32R, stack=st)
            res = sb("res", [P, TT, D], stack=st)
            ln_t = sb("ln_t", [P, 2, 4, P], stack=st)
            stats = sb("stats", [P, TT, 4, 6], stack=st)
            mv = sb("mv", [P, TT, 4], stack=st)
        with ExitStack() as st:
            rx_pad = sb("rx_pad", [P, 2, 2, T + CONV - 1], stack=st)
            conv_y = sb("conv_y", [P, 2, T], stack=st)
        v_h = sb("v_h", [P, TT, DV])
        state = sb("state", [P, 2, DV])
        alpha_cur = sb("alpha_cur", [RANK, DK])
        lr_t = sb("lr_t", [RANK, T])
        lru_c = sb("lru_c", [P, KT])
        lamt = sb("lamt", [P, 4, KT])
        o_sq = sb("o_sq", [P, TT, 4, P])
        lru_a = sb("lru_a", [P, 4, T])
        lru_m = sb("lru_m", [P, 4, T])
        h_lru = sb("h_lru", [P, 4, T])
        ones_dv = sb("ones_dv", [P, P])
        chunk_mask = sb("chunk_mask", [P, 2 * T], BF16)
        q_h = sb("q_h", [P, 2, T])
        k_h = sb("k_h", [P, 2, T])
        bc = sb("bc", [P, 2, T])
        e_pos = sb("e_pos", [P, 2, T])
        e_neg = sb("e_neg", [P, 2, T])
        qk_dec = sb("qk_dec", [P, 2, 2, T])
        k_end = sb("k_end", [P, 2, T])
        k_end_t = sb("k_end_t", [P, TT, DK])
        scores = sb("scores", [P, TT, CHUNK])
        silu_g = sb("silu_g", [P, 4, T])
        rstd = sb("rstd", [P, TT, P])
        a_sq = o_sq[:, :, :, :].rearrange("p t (a b) i -> p (t a) (b i)", b=2)
        o_g = qk_dec[:, :, :, :].rearrange("p a b t -> p (a b) t")

        raw_landed = [sem(f"raw_landed{s}") for s in range(RING)]
        hi_ready, lo_ready, piece_done = sem("hi_ready"), sem("lo_ready"), sem("piece_done")
        corr_out, group_read = sem("corr_out"), sem("group_read")
        x_landed = [sem(f"x_landed{c}") for c in range(4)]
        par_landed, lrw_landed, alpha_landed = sem("par_landed"), sem("lrw_landed"), sem("alpha_landed")
        consts, x_turned, x_hi_out, x_lo_out = sem("consts"), sem("x_turned"), sem("x_hi_out"), sem("x_lo_out")
        lr_hi_ready, lr_lo_ready, lr_done, lr_corr, lr_ready = (
            sem("lr_hi_ready"), sem("lr_lo_ready"), sem("lr_done"), sem("lr_corr"), sem("lr_ready"))
        lam_exp = sem("lam_exp")
        dve_pro, dve_rx, dve_head, dve_ln = sem("dve_pro"), sem("dve_rx"), sem("dve_head"), sem("dve_ln")
        lam_pre = sem("lam_pre")
        conv_out, conv_hi, conv_lo = sem("conv_out"), sem("conv_hi"), sem("conv_lo")
        tap0 = sem("tap0")
        lg_corr, lg_read = sem("lg_corr"), sem("lg_read")
        alpha_done, alpha_out, ls_exp, ls_ln, bc_ready = (
            sem("alpha_done"), sem("alpha_out"), sem("ls_exp"), sem("ls_ln"), sem("bc_ready"))
        gates_ready, x_conv, ix_ready = sem("gates_ready"), sem("x_conv"), sem("ix_ready")
        decay_exp, decay_sq, h_ready = sem("decay_exp"), sem("decay_sq"), sem("h_ready")
        e_pos_ready, e_neg_ready, k_diff, e_end_ready, dec_ready = (
            sem("e_pos_ready"), sem("e_neg_ready"), sem("k_diff"), sem("e_end_ready"), sem("dec_ready"))
        kt_done, kt_out, sc_out, sc_masked = sem("kt_done"), sem("kt_out"), sem("sc_out"), sem("sc_masked")
        v_out, chunk_done, state_ready, o_done = sem("v_out"), sem("chunk_done"), sem("state_ready"), sem("o_done")
        sq_ready, ms_done, og_ready, og_hi, og_lo = (
            sem("sq_ready"), sem("ms_done"), sem("og_ready"), sem("og_hi"), sem("og_lo"))
        act_ready, b_ready, b_hi, b_lo = sem("act_ready"), sem("b_ready"), sem("b_hi"), sem("b_lo")
        gated, merged_ready, ff_ready = sem("gated"), sem("merged_ready"), sem("ff_ready")
        stage_hi, stage_ready = sem("stage_hi"), sem("stage_ready")
        res_landed, tok_landed, z_ready, mv_ready, z_norm = (
            sem("res_landed"), sem("tok_landed"), sem("z_ready"), sem("mv_ready"), sem("z_norm"))
        ln_turned, ln_out, ln_hi, ln_lo = sem("ln_turned"), sem("ln_out"), sem("ln_hi"), sem("ln_lo")
        pool_res, res_step, ln2_landed = sem("pool_res"), sem("res_step"), sem("ln2_landed")
        scaled, out_ready, out_ready_pool, stored = sem("scaled"), sem("out_ready"), sem("out_ready_pool"), sem("stored")
        gap_ready, gap_root, rms_inv, rms_root = sem("gap_ready"), sem("gap_root"), sem("rms_inv"), sem("rms_root")
        table_ready = sem("table_ready")
        ln_inv, ln_root = sem("ln_inv"), sem("ln_root")
        pool_set, mask_ready = sem("pool_set"), sem("mask_ready")

        def pcol(name, i, n=1):
            return par[:, bass.ds(PAR[name] + i, n)]

        block = ctx.enter_context(nc.Block())

        @block.sync
        def _(sp):
            w_in_v = w_in.rearrange("(k p) c -> p k c", p=P)
            for c in range(4):
                sp.dma_start(x_in[:, :, c * 512:(c + 1) * 512],
                             x[:, c * 512:(c + 1) * 512].rearrange("(t p) d -> p t d", p=P)).then_inc(x_landed[c], 16)
            sp.dma_start(par[:, :], params).then_inc(par_landed, 16)

            def load(it, p, source, first=False):
                if not first:
                    sp.wait_ge(lo_ready, SLOTS * it + p - RING + 1)
                s = p % RING
                dst = raw[:, s, :]
                if len(source.shape) == 3:
                    dst = dst.rearrange("p (k c) -> p k c", k=source.shape[1])
                sp.dma_start(dst, source).then_inc(raw_landed[s], 16)

            def columns(w, it, half, col, first=False):
                for q in range(4):
                    load(it, 4 * half + q, w[:, 4 * q:4 * q + 4, bass.ds(col, GROUP)], first)

            rx = lambda j, half: COL_RX + 2 * GROUP * j + GROUP * half
            columns(w_in_v, 0, 0, rx(0, 0), first=True)
            sp.dma_start(lr_raw[:, :, :], w_in_v[:, :, COL_LR:COL_LR + P]).then_inc(lrw_landed, 16)
            columns(w_in_v, 0, 1, rx(0, 1))
            with sp.Fori(1, N_RX) as j:
                columns(w_in_v, j + I_RX, 0, rx(j, 0))
                columns(w_in_v, j + I_RX, 1, rx(j, 1))
            for p in range(SLOTS):
                load(I_LG, p, lru_w[p])
            w_v = w_in.rearrange("(q k p) c -> q p k c", p=P, k=2)
            with sp.Fori(0, HEADS) as j:
                it = 4 * j + I_HEAD
                columns(w_in_v, it, 0, COL_Q + DK * j)
                columns(w_in_v, it, 1, COL_K + DK * j)
                for p in range(SLOTS):
                    load(it + 1, p, w_v[p, :, :, bass.ds(COL_V + DV * j, DV)])
                columns(w_in_v, it + 2, 0, COL_G + DV * j)
                columns(w_in_v, it + 2, 1, COL_G + DV * j + GROUP)
                columns(w_in_v, it + 3, 0, COL_RY + 2 * GROUP * j)
                columns(w_in_v, it + 3, 1, COL_RY + 2 * GROUP * j + GROUP)
            for base, n, w, col in ((I_B, N_B, rnn_o, COL_GB), (I_A, N_A, w_o, COL_GA)):
                w = w.rearrange("(k p) c -> p k c", p=P)
                with sp.Fori(base, base + n) as it:
                    columns(w_in_v, it, 0, GROUP * it + (col - GROUP * base))
                    columns(w, it, 1, GROUP * it - GROUP * base)
            w_rows = w_out.rearrange("(k p) (h c) -> k h p c", p=P, c=PIECE)
            with sp.Fori(0, N_OUT) as j:
                for p in range(SLOTS):
                    load(j + I_OUT, p, w_rows[bass.ds(4 * j + p // 2, 1), p % 2].rearrange("a p c -> (a p) c"))
            w_gu_v = w_gu.rearrange("(k p) c -> p k c", p=P)
            with sp.Fori(0, N_FFN) as j:
                columns(w_gu_v, j + I_FFN, 0, GROUP * j)
                columns(w_gu_v, j + I_FFN, 1, FF + GROUP * j)
            w_rows2 = w_down.rearrange("(k p) (h c) -> k h p c", p=P, c=PIECE)
            with sp.Fori(0, N_DOWN) as j:
                for p in range(SLOTS):
                    load(j + I_DOWN, p, w_rows2[bass.ds(4 * j + p // 2, 1), p % 2].rearrange("a p c -> (a p) c"))
            sp.wait_ge(pool_res, TT)
            sp.dma_start(tok_g1[:, :], ln2_g.to_broadcast([P, D])).then_inc(ln2_landed, 16)
            sp.dma_start(tok_b1[:, :], ln2_b.to_broadcast([P, D])).then_inc(ln2_landed, 16)
            for tt in range(TT):
                for ready, part in ((out_ready, slice(0, LN_DVE)), (out_ready_pool, slice(LN_DVE, D))):
                    sp.wait_ge(ready, tt + 1)
                    sp.dma_start(out[tt * P:(tt + 1) * P, part], res[:, tt, part]).then_inc(stored, 16)
            sp.wait_ge(stored, 16 * 2 * TT)

        @block.tensor
        def _(pe):
            def mm(o, w, m, start, stop):
                return nc.tensor.matmul(o, w, m, start=start, stop=stop)

            def arrived(it, p):
                pe.wait_ge(lo_ready, SLOTS * it + p + 1)

            def tile_product(bank, hi, lo, moving, first, last):
                whole, main = psum[:, bank, :], psum[:, bank, 0:T]
                if first:
                    mm(whole, hi, moving, True, False)
                    return mm(main, lo, moving[:, 0:T], False, False)
                mm(main, lo, moving[:, 0:T], False, False)
                return mm(whole, hi, moving, False, last)

            def piece(it, p, moving, banks):
                arrived(it, p)
                s, q = p % RING, p % 4
                for i in range(4):
                    for c in range(2):
                        w = slice(i * GROUP + c * P, i * GROUP + (c + 1) * P)
                        last = tile_product(banks + c, w_hi[:, s, w], w_lo[:, s, w], moving[:, 4 * q + i, :],
                                            q == 0 and i == 0, q == 3 and i == 3)
                last.then_inc(piece_done, 1)

            def group(it, half, moving, g, after=()):
                if g is not None:
                    pe.wait_ge(group_read, g - 1)
                for q in range(4):
                    piece(it, 4 * half + q, moving, 2 * half)
                    if q < len(after) and after[q]:
                        after[q]()

            def token_tile(p, at, act, banks, n_of, first, last):
                s = p % RING
                for tt in range(TT):
                    hi, lo = act[:, tt * P:(tt + 1) * P], act[:, T + tt * P:T + (tt + 1) * P]
                    for n in range(n_of):
                        bank = banks(tt, n)
                        m = slice(at + n * 512, at + (n + 1) * 512)
                        mm(psum[:, bank, :], hi, w_hi[:, s, m], first, False)
                        mm(psum[:, bank, :], hi, w_lo[:, s, m], False, False)
                        r = mm(psum[:, bank, :], lo, w_hi[:, s, m], False, last)
                return r

            pe.sem_inc(ms_done, FREE)
            pe.wait_ge(consts, 2)
            for q in range(KT // 2):
                if q % 2 == 0:
                    pe.wait_ge(x_landed[q // 2], 16)
                for k in range(2):
                    for tt in range(TT):
                        at = k * T + tt * P
                        r = nc.tensor.transpose(psum[:, q, at:at + P],
                                                x_in[:, tt, (2 * q + k) * P:(2 * q + k + 1) * P], ident[:, :])
                r.then_inc(x_turned, 1)
            pe.wait_ge(x_lo_out, KT // 2)

            group(0, 0, x_t, None)
            group(0, 1, x_t, None)
            with pe.Fori(1, N_RX) as j:
                group(j + I_RX, 0, x_t, 2 * j + G_RX)
                group(j + I_RX, 1, x_t, 2 * j + G_RX + 1)

            pe.wait_ge(lr_lo_ready, 1)
            for kt in range(KT):
                r = tile_product(4, lr_hi[:, kt, :], lr_lo[:, kt, :], x_t[:, kt, :], kt == 0, kt == KT - 1)
            r.then_inc(lr_done, 1)

            for p in range(SLOTS):
                arrived(I_LG, p)
                s, base = p % RING, 4 * (p % 2)
                if p == 0:
                    pe.wait_ge(group_read, G_HEAD)
                if p == 1:
                    pe.wait_ge(lr_ready, 1)
                if p >= 2:
                    pe.wait_ge(lg_read, p - 1)
                pe.wait_ge(conv_lo, FREE + p + 1)
                for kt in range(2):
                    for g in range(4):
                        w = slice(kt * 512 + g * P, kt * 512 + (g + 1) * P)
                        last = tile_product(base + g, w_hi[:, s, w], w_lo[:, s, w], b_t[:, 2 * p + kt, :],
                                            kt == 0, kt == 1)
                last.then_inc(piece_done, 1)
            pe.wait_ge(lg_read, SLOTS)

            with pe.Fori(0, HEADS) as j:
                it, g = 4 * j + I_HEAD, 6 * j + G_HEAD

                def alpha():
                    pe.wait_ge(alpha_landed, 16 * j + 16)
                    pe.wait_ge(o_done, FREE + 2 * j)
                    for c in range(2):
                        r = mm(psum[:, 4, c * T:(c + 1) * T], alpha_cur[:, c * P:(c + 1) * P], lr_t[:, :], True, True)
                    r.then_inc(alpha_done, 1)

                def keys_and_scores():
                    pe.wait_ge(dec_ready, FREE + 3 * j + 3)
                    pe.wait_ge(alpha_out, j + 1)
                    for tt in range(TT):
                        for c in range(2):
                            nc.tensor.transpose(psum[:, 4, tt * DK + c * P:tt * DK + (c + 1) * P],
                                                k_end[:, c, tt * P:(tt + 1) * P], ident[:, :])
                    for n in range(NCHUNK):
                        tt, at = n // 2, CHUNK * (n % 2)
                        tok = slice(n * CHUNK, (n + 1) * CHUNK)
                        for c in range(2):
                            r = mm(psum[at:at + CHUNK, 5, tt * CHUNK:(tt + 1) * CHUNK], qk_dec[:, 1, c, tok],
                                   qk_dec[:, 0, c, tok], c == 0, c == 1)
                    r.then_inc(kt_done, 1)

                def chunk(n):
                    tt, at = n // 2, CHUNK * (n % 2)
                    rows, tok = slice(at, at + CHUNK), slice(n * CHUNK, (n + 1) * CHUNK)
                    if n == 0:
                        pe.wait_ge(kt_out, j + 1)
                        pe.wait_ge(sc_masked, 2 * j + 2)
                        pe.wait_ge(v_out, j + 1)
                    else:
                        pe.wait_ge(state_ready, FREE + 3 * j + n)
                    for b in range(DV // P):
                        o = psum[:, 4 + tt, b * P + at:b * P + at + CHUNK]
                        dv = slice(b * P, (b + 1) * P)
                        if n:
                            mm(o, state[:, 0, dv], qk_dec[:, 0, 0, tok], True, False)
                            mm(o, state[:, 1, dv], qk_dec[:, 0, 1, tok], False, False)
                        r = mm(o, v_h[rows, tt, dv], scores[rows, tt, :], n == 0, True)
                    if n < NCHUNK - 1:
                        for c in range(2):
                            r = mm(psum[:, 6 + c, :], k_end_t[rows, tt, c * P:(c + 1) * P], v_h[rows, tt, :], True, True)
                    r.then_inc(chunk_done, 1)

                def mean_square():
                    pe.wait_ge(sq_ready, j + 1)
                    for b in range(DV // P):
                        r = mm(psum[:, 6, 0:T].rearrange("p (t i) -> p t i", t=TT), ones_dv[:, :], o_sq[:, :, b, :],
                               b == 0, b == DV // P - 1)
                    r.then_inc(ms_done, 1)

                group(it, 0, x_t, g, (alpha,))
                group(it, 1, x_t, g + 1)
                for p in range(SLOTS):
                    arrived(it + 1, p)
                    if p == 0:
                        pe.wait_ge(og_ready, FREE + 2 * j)
                    for i in range(2):
                        r = token_tile(p, i * DV, x_t[:, 2 * p + i, :], lambda tt, n: 6 + tt, 1,
                                       p == 0 and i == 0, p == SLOTS - 1 and i == 1)
                    r.then_inc(piece_done, 1)
                    if p == 4:
                        keys_and_scores()
                group(it + 2, 0, x_t, g + 2, (None, lambda: chunk(0), None, lambda: chunk(1)))
                group(it + 2, 1, x_t, g + 3, (None, lambda: chunk(2), None, lambda: chunk(3)))
                group(it + 3, 0, x_t, g + 4, (None, mean_square))
                group(it + 3, 1, x_t, g + 5)

            for base, gb, n, act in ((I_B, G_B, N_B, b_t), (I_A, G_A, N_A, o_t)):
                with pe.Fori(0, n) as j:
                    group(j + base, 0, x_t, 2 * j + gb)
                    pe.wait_ge(b_lo, FREE + 2 * HEADS)
                    group(j + base, 1, act, 2 * j + gb + 1)

            def token_major(it, done, last_it, first_it):
                for p in range(SLOTS):
                    arrived(it, p)
                    if p % 2 == 0:
                        pe.wait_ge(stage_ready, done + p // 2 + 1)
                    r = token_tile(p, 0, stage[:, p // 2, :], lambda tt, n: 4 * tt + 2 * (p % 2) + n, 2,
                                   first_it and p < 2, last_it and p >= SLOTS - 2)
                    r.then_inc(piece_done, 1)

            pe.wait_ge(group_read, G_FFN)
            token_major(I_OUT, 0, False, True)
            with pe.Fori(1, N_OUT - 1) as j:
                token_major(j + I_OUT, 4 * j, False, False)
            token_major(I_OUT + N_OUT - 1, 4 * (N_OUT - 1), True, False)

            for tt in range(TT):
                pe.wait_ge(z_norm, tt + 1)
                for b in range(4):
                    for i in range(4):
                        kt = 4 * b + i
                        r = nc.tensor.transpose(psum[:, 4 * tt + b, i * P:(i + 1) * P],
                                                res[:, tt, kt * P:(kt + 1) * P], ident[:, :])
                    r.then_inc(ln_turned, 1)
            pe.wait_ge(ln_lo, 8)
            with pe.Fori(0, N_FFN) as j:
                group(j + I_FFN, 0, x_t, 2 * j + G_FFN)
                group(j + I_FFN, 1, x_t, 2 * j + G_FFN + 1)
            pe.wait_ge(group_read, G_END)
            token_major(I_DOWN, 4 * N_OUT, False, True)
            with pe.Fori(1, N_DOWN - 1) as j:
                token_major(j + I_DOWN, 4 * j + 4 * N_OUT, False, False)
            token_major(I_DOWN + N_DOWN - 1, 4 * (N_OUT + N_DOWN - 1), True, False)

        @block.scalar
        def _(act):
            A = nc.scalar.activation

            def split(it, p, ahead=RING):
                s = p % RING
                if ahead:
                    act.wait_ge(piece_done, SLOTS * it + p + 1)
                act.wait_ge(raw_landed[s], 32 * it + 16 * ((p + ahead) // RING + 1))
                A(w_hi[:, s, :], raw[:, s, :], ACT.Copy).then_inc(hi_ready, 1)

            def copy_corr(half):
                A(corr[:, 2 * half:2 * half + 2, :], psum[:, 2 * half:2 * half + 2, T:2 * T], ACT.Copy)\
                    .then_inc(corr_out, 1)

            for q in range(KT // 2):
                act.wait_ge(x_turned, q + 1)
                A(x_t[:, 2 * q:2 * q + 2, 0:T], psum[:, q, :].rearrange("p (k t) -> p k t", k=2), ACT.Copy)\
                    .then_inc(x_hi_out, 1)
                if q % 2:
                    split(0, q // 2, 0)
            act.wait_ge(lrw_landed, 16)
            A(lr_hi[:, :, :], lr_raw[:, :, :], ACT.Copy).then_inc(lr_hi_ready, 1)
            act.wait_ge(lam_pre, 1)
            A(lamt[:, 1, :], lamt[:, 0, :], ACT.Exp, scale=-1.0).then_inc(lam_exp, 1)

            with act.Fori(0, N_RX) as j:
                for p in range(SLOTS):
                    split(j + I_RX, p)
                    if p % 4 == 3:
                        half = p // 4
                        copy_corr(half)
                        act.wait_ge(group_read, 2 * j + half + 1)
                        act.wait_ge(conv_lo, FREE + 2 * j + half)
                        for c in range(2):
                            t = 4 * j + 2 * half + c
                            r = A(conv_y[:, c, :], rx_pad[:, half, c, 0:T], ACT.Identity,
                                  bias=pcol("conv_b", t), scale=pcol("conv_w", t))
                            r.then_inc(tap0, 1)
                    if p in (5, 7):
                        half = p // 7
                        act.wait_ge(conv_out, 2 * j + half + 1)
                        A(b_t[:, bass.ds(4 * j + 2 * half, 2), 0:T], conv_y[:, :, :], ACT.Copy).then_inc(conv_hi, 1)

            act.wait_ge(lr_done, 1)
            A(corr[0:RANK, 0, :], psum[0:RANK, 4, T:2 * T], ACT.Copy).then_inc(lr_corr, 1)

            def gates_sigmoid(p):
                A(gates[:, 2 * p:2 * p + 2, :], gates[:, 2 * p:2 * p + 2, :], ACT.Sigmoid).then_inc(gates_ready, 1)

            for p in range(SLOTS):
                split(I_LG, p)
                if p == 0:
                    act.wait_ge(lr_ready, 1)
                if p > 0:
                    act.wait_ge(lg_read, p)
                A(corr[:, :, :], psum[:, 4 * (p % 2):4 * (p % 2) + 4, T:2 * T], ACT.Copy).then_inc(lg_corr, 1)
                if p > 0:
                    gates_sigmoid(p - 1)
            act.wait_ge(lg_read, SLOTS)
            gates_sigmoid(SLOTS - 1)

            with act.Fori(0, HEADS) as j:
                it = 4 * j + I_HEAD

                def decays(m):
                    if m == 0:
                        act.wait_ge(h_ready, FREE + j)
                        act.wait_ge(gates_ready, SLOTS)
                    for f, to in ((ACT.Exp, lru_a), (ACT.Tanh, lru_m)):
                        for c in (2 * m, 2 * m + 1):
                            t = bass.ds(4 * j + c, 1)
                            A(to[:, c, :], gates[:, t, 0:T].rearrange("p a t -> p (a t)"), f, scale=lru_c[:, t])\
                                .then_inc(decay_exp, 1)

                for p in range(SLOTS):
                    split(it, p)
                    if p < 2:
                        decays(p)
                    if p == 4:
                        act.wait_ge(ms_done, FREE + j)
                        act.wait_ge(decay_exp, 8 * j + 8)
                        A(a_sq, lru_a[:, :, :], ACT.Square).then_inc(decay_sq, 1)
                    if p == 2:
                        act.wait_ge(alpha_out, j + 1)
                        A(e_neg[:, :, :], e_neg[:, :, :], ACT.Exp, scale=-1.0).then_inc(ls_exp, 1)
                    if p % 4 == 3:
                        copy_corr(p // 4)
                    if p == 6:
                        act.wait_ge(ls_exp, j + 1)
                        A(e_neg[:, :, :], e_neg[:, :, :], ACT.Ln, bias=one_col[:, 0:1]).then_inc(ls_ln, 1)
                for p in range(SLOTS):
                    if p == 0:
                        act.wait_ge(bc_ready, j + 1)
                        A(e_pos[:, :, :], bc[:, :, :], ACT.Exp, scale=1.0 / TAU).then_inc(e_pos_ready, 1)
                        A(e_neg[:, :, :], bc[:, :, :], ACT.Exp, scale=-1.0 / TAU).then_inc(e_neg_ready, 1)
                    if p == 1:
                        act.wait_ge(k_diff, FREE + j + 1)
                        A(k_end[:, :, :], k_end[:, :, :], ACT.Exp, scale=-1.0 / TAU).then_inc(e_end_ready, 1)
                    if p == 3:
                        act.wait_ge(gap_ready, j + 1)
                        A(lru_m[:, :, :], lru_m[:, :, :], ACT.Sqrt, scale=-1.0).then_inc(gap_root, 1)
                    split(it + 1, p)
                    if p == 6:
                        act.wait_ge(kt_done, j + 1)
                        A(scores[:, :, :], psum[:, 5, 0:2 * CHUNK].rearrange("p (t i) -> p t i", t=TT), ACT.Copy)\
                            .then_inc(sc_out, 1)
                        A(k_end_t[:, :, :], psum[:, 4, :].rearrange("p (t c) -> p t c", t=TT), ACT.Copy)\
                            .then_inc(kt_out, 1)
                    if p == 7:
                        A(v_h[:, :, :], psum[:, 6:8, :], ACT.Copy).then_inc(v_out, 1)
                for p in range(SLOTS):
                    split(it + 2, p)
                    if p % 4 == 3:
                        half = p // 4
                        copy_corr(half)
                        act.wait_ge(group_read, 6 * j + G_HEAD + 3 + half)
                        if half == 0:
                            act.wait_ge(og_ready, FREE + 2 * j)
                        A(silu_g[:, 2 * half:2 * half + 2, :], gsum[:, :, :], ACT.Silu).then_inc(act_ready, 1)
                for p in range(SLOTS):
                    if p == 5:
                        act.wait_ge(og_ready, FREE + 2 * j + 2)
                    split(it + 3, p)
                    if p == 0:
                        act.wait_ge(chunk_done, 4 * j + 4)
                        act.wait_ge(h_ready, FREE + j + 1)
                        A(o_sq[:, :, :, :], psum[:, 4:6, :].rearrange("p t (b i) -> p t b i", b=4), ACT.Square).then_inc(sq_ready, 1)
                    if p == 2:
                        act.wait_ge(rms_inv, j + 1)
                        A(rstd[:, :, :], rstd[:, :, :], ACT.Sqrt).then_inc(rms_root, 1)
                    if p == 5:
                        A(o_t[:, bass.ds(4 * j, 4), 0:T], o_g, ACT.Copy).then_inc(og_hi, 1)
                    if p % 4 == 3:
                        half = p // 4
                        copy_corr(half)
                        act.wait_ge(group_read, 6 * j + G_HEAD + 5 + half)
                        A(gsum[:, :, :], gsum[:, :, :], ACT.Gelu_apprx_tanh).then_inc(act_ready, 1)
                        act.wait_ge(b_ready, FREE + 2 * j + half + 1)
                        A(b_t[:, bass.ds(4 * j + 2 * half, 2), 0:T], gsum[:, :, :], ACT.Copy).then_inc(b_hi, 1)

            def stage_tile(m, source):
                A(stage[:, m, 0:T], source, ACT.Copy).then_inc(stage_hi, 1)

            A(scratch[:, 0:1], one_col[:, :], ACT.Sigmoid).then_inc(table_ready, 1)
            for k, base in enumerate((I_B, I_A)):
                with act.Fori(0, N_B) as j:
                    for p in range(SLOTS):
                        split(j + base, p)
                        if p == 3:
                            copy_corr(0)
                            act.wait_ge(group_read, 2 * j + G_B + 2 * k * N_B + 1)
                            A(gsum[:, :, :], gsum[:, :, :], ACT.Sigmoid).then_inc(act_ready, 1)
                        if p == 7:
                            copy_corr(1)
            act.wait_ge(piece_done, SLOTS * I_OUT)
            act.dma_start(res[:, :, :], x.rearrange("(t p) d -> p t d", p=P)).then_inc(res_landed, 16)
            act.dma_start(tok_g1[:, :], ln1_g.to_broadcast([P, D])).then_inc(tok_landed, 16)
            act.dma_start(tok_b1[:, :], ln1_b.to_broadcast([P, D])).then_inc(tok_landed, 16)
            act.wait_ge(merged_ready, FREE + 2 * N_B)
            for m in range(4):
                stage_tile(m, merged[:, m, :])

            def token_major(it, j, source, last_it):
                for p in range(SLOTS):
                    if not (last_it and p >= SLOTS - RING and source is h_ff):
                        split(it, p)
                    if p % 2 == 1 and not last_it:
                        m = p // 2
                        act.wait_ge(piece_done, SLOTS * it + p + 1)
                        stage_tile(m, source[:, bass.ds(4 * j + 4 + m, 1), :].rearrange("p a t -> p (a t)"))

            with act.Fori(0, N_OUT - 1) as j:
                token_major(j + I_OUT, j, merged, False)
            token_major(I_OUT + N_OUT - 1, 0, merged, True)

            for tt in range(TT):
                act.wait_ge(ln_inv, tt + 1)
                A(mv[:, tt, 2:3], mv[:, tt, 2:3], ACT.Sqrt).then_inc(ln_root, 1)
                act.wait_ge(mv_ready, tt + 1)
                A(res[:, tt, :], res[:, tt, :], ACT.Identity, bias=mv[:, tt, 3:4], scale=mv[:, tt, 2:3])\
                    .then_inc(z_norm, 1)
            for n in range(8):
                tt, b = n // 4, n % 4
                act.wait_ge(ln_out, n + 1)
                A(x_t[:, 4 * b:4 * b + 4, tt * P:(tt + 1) * P], ln_t[:, n % 2, :, :], ACT.Copy).then_inc(ln_hi, 1)

            A(scratch[:, 1:2], scratch[:, 0:1], ACT.Silu).then_inc(table_ready, 1)
            with act.Fori(0, N_FFN) as j:
                for p in range(SLOTS):
                    split(j + I_FFN, p)
                    if p == 3:
                        copy_corr(0)
                        act.wait_ge(group_read, 2 * j + G_FFN + 1)
                        act.wait_ge(ff_ready, FREE + j)
                        A(yb[:, :, :], gsum[:, :, :], ACT.Silu).then_inc(act_ready, 1)
                    if p == 7:
                        copy_corr(1)
            act.wait_ge(ff_ready, FREE + N_FFN)
            for m in range(4):
                stage_tile(m, h_ff[:, m, :])
            with act.Fori(0, N_DOWN - 1) as j:
                token_major(j + I_DOWN, j, h_ff, False)
            token_major(I_DOWN + N_DOWN - 1, 0, h_ff, True)
            for tt in range(TT):
                act.wait_ge(ln_inv, TT + tt + 1)
                A(mv[:, tt, 2:3], mv[:, tt, 2:3], ACT.Sqrt).then_inc(ln_root, 1)
                act.wait_ge(mv_ready, TT + tt + 1)
                A(res[:, tt, :], res[:, tt, :], ACT.Identity, bias=mv[:, tt, 3:4], scale=mv[:, tt, 2:3])\
                    .then_inc(z_norm, 1)

        @block.vector
        def _(dve):
            tt_op, ts_op, stt = nc.vector.tensor_tensor, nc.vector.tensor_scalar, nc.vector.scalar_tensor_tensor

            def split(it, p, ahead=RING):
                s = p % RING
                dve.wait_ge(hi_ready, SLOTS * it + p + ahead + 1)
                tt_op(w_lo[:, s, :], raw[:, s, :], w_hi[:, s, :].bitcast(F32), ALU.subtract).then_inc(lo_ready, 1)

            def group_sum(to, half, g):
                dve.wait_ge(corr_out, g + 1)
                tt_op(to, psum[:, 2 * half:2 * half + 2, 0:T], corr[:, 2 * half:2 * half + 2, :], ALU.add)\
                    .then_inc(group_read, 1)

            for free in (state_ready, dec_ready, k_diff, o_done, og_ready, h_ready, b_lo, conv_lo, merged_ready,
                         ff_ready, og_lo, b_ready):
                dve.sem_inc(free, FREE)
            pro = Steps(dve, dve_pro)
            pro.step(nc.vector.memset(rx_pad[:, :, :, 0:CONV - 1], 0.0))
            pro.step(nc.vector.memset(one_col[:, :], 1.0))
            for q in range(KT // 2):
                dve.wait_ge(x_hi_out, q + 1)
                tt_op(x_t[:, 2 * q:2 * q + 2, T:2 * T], psum[:, q, :].rearrange("p (k t) -> p k t", k=2),
                      x_t[:, 2 * q:2 * q + 2, 0:T].bitcast(F32), ALU.subtract).then_inc(x_lo_out, 1)
                if q % 2:
                    split(0, q // 2, 0)
            dve.wait_ge(lr_hi_ready, 1)
            tt_op(lr_lo[:, :, :], lr_raw[:, :, :], lr_hi[:, :, :].bitcast(F32), ALU.subtract).then_inc(lr_lo_ready, 1)
            dve.wait_ge(par_landed, 16)
            lam = pcol("lambda", 0, KT)
            stt(lamt[:, 0, :], lam, -1.0, lam, ALU.mult, ALU.max).then_inc(lam_pre, 1)
            dve.wait_ge(lam_exp, 1)
            y, s_, z_, acc = lamt[:, 1, :], lamt[:, 2, :], lamt[:, 3, :], lru_c[:, :]
            pro.step(ts_op(s_, y, 2.0, None, ALU.add))
            pro.wait()
            pro.step(nc.vector.reciprocal(s_, s_))
            pro.wait()
            pro.step(tt_op(s_, s_, y, ALU.mult))
            pro.wait()
            pro.step(tt_op(z_, s_, s_, ALU.mult))
            pro.step(nc.vector.memset(acc, 1.0 / (2 * LOG1P_TERMS - 1)))
            for n in range(LOG1P_TERMS - 2, -1, -1):
                pro.wait()
                pro.step(tt_op(acc, acc, z_, ALU.mult))
                pro.wait()
                pro.step(ts_op(acc, acc, 1.0 / (2 * n + 1), None, ALU.add))
            pro.wait()
            pro.step(tt_op(acc, acc, s_, ALU.mult))
            pro.step(ts_op(y, lam, -1.0, 0.0, ALU.mult, ALU.max))
            pro.wait()
            pro.step(ts_op(y, y, -LRU_C, None, ALU.mult))
            pro.wait()
            pro.step(stt(acc, acc, -2.0 * LRU_C, y, ALU.mult, ALU.add))
            pro.wait()

            per = 2 * 2 * (CONV - 2)
            with dve.Fori(0, N_RX) as j:
                own = Steps(dve, dve_rx, j, per)
                for p in range(SLOTS):
                    split(j + I_RX, p)
                    if p % 4 == 3:
                        half = p // 4
                        b = 2 * j + half
                        dve.wait_ge(corr_out, b + 1)
                        tt_op(rx_pad[:, half, :, CONV - 1:], psum[:, 2 * half:2 * half + 2, 0:T],
                              corr[:, 2 * half:2 * half + 2, :], ALU.add).then_inc(group_read, 1)
                        for k in range(1, CONV):
                            if k == 1:
                                dve.wait_ge(tap0, 2 * b + 2)
                            else:
                                own.wait()
                            for c in range(2):
                                w = par[:, bass.ds(4 * j + PAR["conv_w"] + k * KT + 2 * half + c, 1)]
                                r = stt(conv_y[:, c, :], rx_pad[:, half, c, k:k + T], w, conv_y[:, c, :],
                                        ALU.mult, ALU.add)
                                if k < CONV - 1:
                                    own.step(r)
                        r.then_inc(conv_out, 1)
                        dve.wait_ge(conv_hi, b + 1)
                        tile = bass.ds(4 * j + 2 * half, 2)
                        tt_op(b_t[:, tile, T:2 * T], conv_y[:, :, :], b_t[:, tile, 0:T].bitcast(F32), ALU.subtract)\
                            .then_inc(conv_lo, 1)
                own.end()

            dve.wait_ge(lr_corr, 1)
            tt_op(lr_t[:, :], psum[0:RANK, 4, 0:T], corr[0:RANK, 0, :], ALU.add).then_inc(lr_ready, 1)
            for p in range(SLOTS):
                split(I_LG, p)
                dve.wait_ge(lg_corr, p + 1)
                for g, name in enumerate(("b_a", "b_x")):
                    for c in range(2):
                        t = 2 * p + c
                        r = stt(gates[:, t, g * T:(g + 1) * T], psum[:, 4 * (p % 2) + 2 * g + c, 0:T],
                                pcol(name, t), corr[:, 2 * g + c, :], ALU.add, ALU.add)
                r.then_inc(lg_read, 1)

            per = 2 + 1 + 1 + 1
            with dve.Fori(0, HEADS) as j:
                it, g = 4 * j + I_HEAD, 6 * j + G_HEAD
                own = Steps(dve, dve_head, j, per)

                def lru_scan():
                    dve.wait_ge(gap_root, j + 1)
                    dve.wait_ge(b_ready, FREE + 2 * j)
                    dve.wait_ge(ix_ready, SLOTS)
                    own.step(tt_op(h_lru[:, :, :], gates[:, bass.ds(4 * j, 4), T:2 * T], lru_m[:, :, :], ALU.mult))
                    own.wait()
                    for c in range(4):
                        r = nc.vector.tensor_tensor_scan(h_lru[:, c, :], lru_a[:, c, :], h_lru[:, c, :], 0.0,
                                                         ALU.mult, ALU.add)
                    r.then_inc(h_ready, 1)

                for p in range(SLOTS):
                    split(it, p)
                    if p == 1:
                        dve.wait_ge(alpha_done, j + 1)
                        dve.wait_ge(state_ready, FREE + 3 * j)
                        dve.wait_ge(dec_ready, FREE + 3 * j)
                        for c in range(2):
                            own.step(ts_op(e_pos[:, c, :], psum[:, 4, c * T:(c + 1) * T], pcol("b_alpha", 2 * j + c), None,
                                           ALU.add))
                        own.wait()
                        stt(e_neg[:, :, :], e_pos[:, :, :], -1.0, e_pos[:, :, :], ALU.mult, ALU.max).then_inc(alpha_out, 1)
                    if p == 3:
                        group_sum(q_h[:, :, :], 0, g)
                    if p == 5:
                        dve.wait_ge(decay_sq, j + 1)
                        stt(lru_m[:, :, :], a_sq, 1.0, lru_m[:, :, :], ALU.add, ALU.mult).then_inc(gap_ready, 1)
                    if p == 7:
                        group_sum(k_h[:, :, :], 1, g + 1)
                        dve.wait_ge(ls_ln, j + 1)
                        own.step(stt(e_pos[:, :, :], e_pos[:, :, :], 0.0, e_neg[:, :, :], ALU.min, ALU.subtract))
                        own.wait()
                        dve.wait_ge(mask_ready, 1)
                        dve.wait_ge(k_diff, FREE + j)
                        nc.vector.tensor_tensor_scan(bc[:, :, :].rearrange("p c t -> p (c t)"), chunk_mask[:, :],
                                                     e_pos[:, :, :].rearrange("p c t -> p (c t)"), 0.0,
                                                     ALU.mult, ALU.add).then_inc(bc_ready, 1)
                        dve.wait_ge(bc_ready, j + 1)
                        v = lambda t: t[:, :, :].rearrange("p c (n t) -> p (c n) t", t=CHUNK)
                        tt_op(v(k_end), v(bc), v(bc)[:, :, CHUNK - 1:CHUNK].to_broadcast([P, 2 * NCHUNK, CHUNK]),
                              ALU.subtract).then_inc(k_diff, 1)
                for p in range(SLOTS):
                    split(it + 1, p)
                    if p == 1:
                        dve.wait_ge(e_pos_ready, j + 1)
                        dve.wait_ge(group_read, g + 2)
                        dve.wait_ge(og_lo, FREE + j)
                        stt(qk_dec[:, 0, :, :], q_h[:, :, :], DK ** -0.5, e_pos[:, :, :], ALU.mult, ALU.mult)\
                            .then_inc(dec_ready, 1)
                        dve.wait_ge(e_neg_ready, j + 1)
                        tt_op(qk_dec[:, 1, :, :], k_h[:, :, :], e_neg[:, :, :], ALU.mult).then_inc(dec_ready, 1)
                    if p == 2:
                        dve.wait_ge(e_end_ready, j + 1)
                        tt_op(k_end[:, :, :], k_h[:, :, :], k_end[:, :, :], ALU.mult).then_inc(dec_ready, 1)
                    if p == 4:
                        lru_scan()
                for p in range(SLOTS):
                    if p in (2, 4, 6):
                        n = p // 2 - 1
                        dve.wait_ge(chunk_done, 4 * j + n + 1)
                        dve.wait_ge(state_ready, FREE + 3 * j + n)
                        for c in range(2):
                            if n == 0:
                                r = nc.vector.tensor_copy(state[:, c, :], psum[:, 6 + c, :])
                            else:
                                at = n * CHUNK + CHUNK - 1
                                r = stt(state[:, c, :], state[:, c, :], e_pos[:, c, at:at + 1], psum[:, 6 + c, :],
                                        ALU.mult, ALU.add)
                        r.then_inc(state_ready, 1)
                    split(it + 2, p)
                    if p % 4 == 3:
                        half = p // 4
                        if half == 0:
                            dve.wait_ge(b_lo, FREE + 2 * j)
                        else:
                            dve.wait_ge(act_ready, 4 * j + 1)
                        group_sum(gsum[:, :, :], half, g + 2 + half)
                for p in range(SLOTS):
                    split(it + 3, p)
                    if p == 2:
                        dve.wait_ge(ms_done, FREE + j + 1)
                        own.step(ts_op(rstd[:, :, :], psum[:, 6, 0:T].rearrange("p (t i) -> p t i", t=TT), EPS, None,
                                       ALU.add))
                        own.wait()
                        nc.vector.reciprocal(rstd[:, :, :], rstd[:, :, :]).then_inc(rms_inv, 1)
                    if p == 4:
                        dve.wait_ge(rms_root, j + 1)
                        for tt in range(TT):
                            r = tt_op(o_g[:, :, tt * P:(tt + 1) * P], psum[:, 4 + tt, :].rearrange("p (b i) -> p b i", b=4),
                                      rstd[:, tt:tt + 1, :].to_broadcast([P, 4, P]), ALU.mult)
                            r.then_inc(o_done, 1)
                        dve.wait_ge(o_done, FREE + 2 * j + 2)
                        dve.wait_ge(act_ready, 4 * j + 2)
                        for b in range(4):
                            r = stt(o_g[:, b, :], o_g[:, b, :], pcol("norm_g", b), silu_g[:, b, :], ALU.mult, ALU.mult)
                            if b % 2:
                                r.then_inc(og_ready, 1)
                    if p == 6:
                        dve.wait_ge(og_hi, j + 1)
                        tile = bass.ds(4 * j, 4)
                        tt_op(o_t[:, tile, T:2 * T], o_g, o_t[:, tile, 0:T].bitcast(F32), ALU.subtract)\
                            .then_inc(og_lo, 1)
                    if p % 4 == 3:
                        half = p // 4
                        dve.wait_ge(act_ready, 4 * j + 2 + half)
                        dve.wait_ge(b_lo, FREE + 2 * j + half)
                        group_sum(gsum[:, :, :], half, g + 4 + half)
                        dve.wait_ge(act_ready, 4 * j + 3 + half)
                        dve.wait_ge(h_ready, FREE + j + 1)
                        tt_op(gsum[:, :, :], gsum[:, :, :], h_lru[:, 2 * half:2 * half + 2, :], ALU.mult)\
                            .then_inc(b_ready, 1)
                        dve.wait_ge(b_hi, 2 * j + half + 1)
                        tile = bass.ds(4 * j + 2 * half, 2)
                        tt_op(b_t[:, tile, T:2 * T], gsum[:, :, :], b_t[:, tile, 0:T].bitcast(F32), ALU.subtract)\
                            .then_inc(b_lo, 1)
                own.end()

            dve.wait_ge(b_lo, FREE + 2 * HEADS)
            for k, base in enumerate((I_B, I_A)):
                gb = G_B + 2 * k * N_B
                with dve.Fori(0, N_B) as j:
                    for p in range(SLOTS):
                        split(j + base, p)
                        if p == 3:
                            dve.wait_ge(merged_ready, FREE + j + k * N_B)
                            group_sum(gsum[:, :, :], 0, 2 * j + gb)
                        if p == 7:
                            group_sum(yb[:, :, :], 1, 2 * j + gb + 1)
                            dve.wait_ge(group_read, 2 * j + gb + 2)
                            dve.wait_ge(act_ready, j + 4 * HEADS + k * N_B + 1)
                            to = merged[:, bass.ds(2 * j, 2), :]
                            if k == 0:
                                tt_op(to, gsum[:, :, :], yb[:, :, :], ALU.mult).then_inc(merged_ready, 1)
                            else:
                                tt_op(yb[:, :, :], gsum[:, :, :], yb[:, :, :], ALU.mult).then_inc(gated, 1)
                                dve.wait_ge(gated, j + 1)
                                tt_op(to, to, yb[:, :, :], ALU.add).then_inc(merged_ready, 1)

            def stage_tile(n, m, source):
                dve.wait_ge(stage_hi, n + 1)
                tt_op(stage[:, m, T:2 * T], source, stage[:, m, 0:T].bitcast(F32), ALU.subtract)\
                    .then_inc(stage_ready, 1)

            def token_major(it, j, first_tile, source, last_it):
                for p in range(SLOTS):
                    if not (last_it and p >= SLOTS - RING and source is h_ff):
                        split(it, p)
                    if p % 2 == 1 and not last_it:
                        m = p // 2
                        stage_tile(4 * j + 4 + m + first_tile, m,
                                   source[:, bass.ds(4 * j + 4 + m, 1), :].rearrange("p a t -> p (a t)"))

            def norm_stats(n, tt, end):
                own = Steps(dve, dve_ln)
                own.n = n
                for b in range(4):
                    dve.wait_ge(piece_done, SLOTS * end - 1 + b // 2)
                    z = res[:, tt, b * 512:(b + 1) * 512]
                    if end == I_FFN:
                        own.step(stt(z, z, ALPHA, psum[:, 4 * tt + b, :], ALU.mult, ALU.add))
                    else:
                        own.step(tt_op(z, z, psum[:, 4 * tt + b, :], ALU.add))
                    own.wait()
                    own.step(nc.vector.bn_stats(stats[:, tt, b, :], z))
                own.wait()
                own.step(nc.vector.bn_aggr(mv[:, tt, 0:2], stats[:, tt, :, :].rearrange("p b s -> p (b s)")))
                own.wait()
                own.step(ts_op(mv[:, tt, 2:3], mv[:, tt, 1:2], EPS, None, ALU.add))
                own.wait()
                nc.vector.reciprocal(mv[:, tt, 2:3], mv[:, tt, 2:3]).then_inc(ln_inv, 1)
                dve.wait_ge(ln_root, (0 if end == I_FFN else TT) + tt + 1)
                stt(mv[:, tt, 3:4], mv[:, tt, 0:1], -1.0, mv[:, tt, 2:3], ALU.mult, ALU.mult).then_inc(mv_ready, 1)
                return own.n

            dve.wait_ge(merged_ready, FREE + 2 * N_B)
            for m in range(4):
                stage_tile(m, m, merged[:, m, :])
            with dve.Fori(0, N_OUT - 1) as j:
                token_major(j + I_OUT, j, 0, merged, False)
            token_major(I_OUT + N_OUT - 1, 0, 0, merged, True)

            dve.wait_ge(res_landed, 16)
            n_ln = norm_stats(0, 0, I_FFN)
            n_ln = norm_stats(n_ln, 1, I_FFN)

            def ln_lo_part(n):
                tt, b = n // 4, n % 4
                dve.wait_ge(ln_hi, n + 1)
                tt_op(x_t[:, 4 * b:4 * b + 4, T + tt * P:T + (tt + 1) * P], ln_t[:, n % 2, :, :],
                      x_t[:, 4 * b:4 * b + 4, tt * P:(tt + 1) * P].bitcast(F32), ALU.subtract).then_inc(ln_lo, 1)

            for n in range(8):
                tt, b = n // 4, n % 4
                dve.wait_ge(ln_turned, n + 1)
                if n >= 2:
                    dve.wait_ge(ln_lo, n - 1)
                for i in range(4):
                    r = ts_op(ln_t[:, n % 2, i, :], psum[:, 4 * tt + b, i * P:(i + 1) * P], pcol("ln1_g", 4 * b + i),
                              pcol("ln1_b", 4 * b + i), ALU.mult, ALU.add)
                r.then_inc(ln_out, 1)
                if n:
                    ln_lo_part(n - 1)
            ln_lo_part(7)

            with dve.Fori(0, N_FFN) as j:
                for p in range(SLOTS):
                    split(j + I_FFN, p)
                    if p == 3:
                        dve.wait_ge(ff_ready, FREE + j)
                        group_sum(gsum[:, :, :], 0, 2 * j + G_FFN)
                    if p == 7:
                        dve.wait_ge(act_ready, j + 4 * HEADS + 2 * N_B + 1)
                        group_sum(gsum[:, :, :], 1, 2 * j + G_FFN + 1)
                        dve.wait_ge(group_read, 2 * j + G_FFN + 2)
                        tt_op(h_ff[:, bass.ds(2 * j, 2), :], gsum[:, :, :], yb[:, :, :], ALU.mult)\
                            .then_inc(ff_ready, 1)
            dve.wait_ge(ff_ready, FREE + N_FFN)
            for m in range(4):
                stage_tile(4 * N_OUT + m, m, h_ff[:, m, :])
            with dve.Fori(0, N_DOWN - 1) as j:
                token_major(j + I_DOWN, j, 4 * N_OUT, h_ff, False)
            token_major(I_DOWN + N_DOWN - 1, 0, 0, h_ff, True)

            dve.wait_ge(pool_res, TT)
            dve.wait_ge(mv_ready, TT)
            n_ln = norm_stats(n_ln, 0, ITERS)
            n_ln = norm_stats(n_ln, 1, ITERS)
            dve.wait_ge(ln2_landed, 32)
            for tt in range(TT):
                dve.wait_ge(z_norm, TT + tt + 1)
                o = res[:, tt, 0:LN_DVE]
                tt_op(o, o, tok_g1[:, 0:LN_DVE], ALU.mult).then_inc(scaled, 1)
                dve.wait_ge(scaled, tt + 1)
                tt_op(o, o, tok_b1[:, 0:LN_DVE], ALU.add).then_inc(out_ready, 1)

        @block.gpsimd
        def _(pool):
            pool.memset(ident[:, :], 0.0).then_inc(pool_set, 1)
            pool.memset(ones_dv[:, :], 1.0 / DV).then_inc(consts, 1)
            pool.memset(chunk_mask[:, :], 1.0).then_inc(pool_set, 1)
            pool.wait_ge(pool_set, 2)
            pool.affine_select(out=ident[:, :], in_=ident[:, :], compare_op=ALU.not_equal, fill=1.0, base=0,
                               pattern=[[-1, P]], channel_multiplier=1).then_inc(consts, 1)
            pool.memset(chunk_mask[:, :].rearrange("p (n t) -> p n t", t=CHUNK)[:, :, 0:1], 0.0).then_inc(mask_ready, 1)
            for p in range(SLOTS):
                two, part = slice(2 * p, 2 * p + 2), slice(2 * (p % 2), 2 * (p % 2) + 2)
                pool.wait_ge(conv_lo, FREE + p + 1)
                if p > 0:
                    pool.wait_ge(ix_ready, p)
                pool.tensor_tensor(h_lru[:, part, :], b_t[:, two, 0:T].bitcast(F32), b_t[:, two, T:2 * T].bitcast(F32),
                                   ALU.add).then_inc(x_conv, 1)
                pool.wait_ge(x_conv, p + 1)
                pool.wait_ge(gates_ready, p + 1)
                pool.tensor_tensor(gates[:, two, T:2 * T], gates[:, two, T:2 * T], h_lru[:, part, :], ALU.mult)\
                    .then_inc(ix_ready, 1)
            pool.wait_ge(ix_ready, SLOTS)
            for j in range(HEADS):
                if j > 0:
                    pool.wait_ge(alpha_done, j)
                pool.dma_start(alpha_cur[:, :], w_alpha[:, DK * j:DK * (j + 1)]).then_inc(alpha_landed, 16)
                pool.wait_ge(sc_out, j + 1)
                for half in range(2):
                    s = scores[CHUNK * half:CHUNK * (half + 1), :, :]
                    pool.affine_select(out=s, in_=s, compare_op=ALU.is_ge, fill=0.0, base=0,
                                       pattern=[[0, TT], [1, CHUNK]], channel_multiplier=-1).then_inc(sc_masked, 1)
            pool.wait_ge(tok_landed, 32)
            pool.wait_ge(ln_turned, 8)
            for tt in range(TT):
                z = res[:, tt, :]
                pool.tensor_tensor(z, z, tok_g1[:, :], ALU.mult).then_inc(res_step, 1)
                pool.wait_ge(res_step, 2 * tt + 1)
                pool.tensor_tensor(z, z, tok_b1[:, :], ALU.add).then_inc(res_step, 1)
                pool.wait_ge(res_step, 2 * tt + 2)
                pool.tensor_scalar(z, z, ALPHA, None, ALU.mult).then_inc(pool_res, 1)
            pool.wait_ge(ln2_landed, 32)
            for tt in range(TT):
                pool.wait_ge(z_norm, TT + tt + 1)
                o = res[:, tt, LN_DVE:D]
                pool.tensor_tensor(o, o, tok_g1[:, LN_DVE:D], ALU.mult).then_inc(res_step, 1)
                pool.wait_ge(res_step, 2 * TT + tt + 1)
                pool.tensor_tensor(o, o, tok_b1[:, LN_DVE:D], ALU.add).then_inc(out_ready_pool, 1)


def kernel(x, w_in, gla_w_alpha, gla_b_alpha, gla_norm_g, gla_w_o, conv_w, conv_b, lru_w_a, lru_b_a, lru_w_x, lru_b_x,
           lru_lambda, rnn_w_o, w_out, ln1_g, ln1_b, w_gate_up, w_down, ln2_g, ln2_b):
    import concourse.bacc as bacc
    from concourse.bass_utils import run_bass_kernel_spmd

    def tiles(a):
        return np.asarray(a).reshape(-1, P).T

    params = np.concatenate([tiles(a) for a in (conv_w, conv_b, lru_b_a, lru_b_x, lru_lambda, gla_b_alpha,
                                                gla_norm_g, ln1_g, ln1_b)], axis=1)
    lru_w = np.stack([np.asarray(a)[0].reshape(8, 2, P, DK) for a in (lru_w_a, lru_w_x)], axis=3)
    lru_w = lru_w.transpose(0, 2, 1, 3, 4).reshape(8, P, PIECE)
    arrays = {
        "x": np.asarray(x)[0], "w_in": np.asarray(w_in)[0], "w_alpha": np.asarray(gla_w_alpha)[0],
        "w_o": np.asarray(gla_w_o)[0], "lru_w": lru_w, "rnn_o": np.asarray(rnn_w_o)[0],
        "w_out": np.asarray(w_out)[0], "w_gu": np.asarray(w_gate_up)[0], "w_down": np.asarray(w_down)[0],
        "params": params, "ln1_g": np.asarray(ln1_g), "ln1_b": np.asarray(ln1_b),
        "ln2_g": np.asarray(ln2_g), "ln2_b": np.asarray(ln2_b),
    }
    nc = bacc.Bacc("TRN2", target_bir_lowering=False, num_devices=1)
    arrays = {k: np.ascontiguousarray(a) for k, a in arrays.items()}
    aps = {k: nc.dram_tensor(k, a.shape, mybir.dt.from_np(a.dtype), kind="ExternalInput").ap()
           for k, a in arrays.items()}
    out = nc.dram_tensor("out", (T, D), F32, kind="ExternalOutput").ap()
    build(nc, out=out, **aps)
    r = run_bass_kernel_spmd(nc, [arrays], core_ids=[0])
    return r.results[0]["out"].reshape(1, T, D)
```

```python
from contextlib import ExitStack

import numpy as np

import concourse.bass as bass
from concourse import mybir

F32 = mybir.dt.float32
F32R = mybir.dt.float32r
BF16 = mybir.dt.bfloat16
ALU = mybir.AluOpType
ACT = mybir.ActivationFunctionType

P = 128
D = 2048
T = 256
TT = T // P
KT = D // P
HEADS = 4
DK = 256
DV = 512
CHUNK = 64
NCHUNK = T // CHUNK
RANK = 16
TAU = 16.0
LRU_C = 8.0
CONV = 4
FF = 5632
ALPHA = 2 ** 0.25
EPS = 1e-5
QUARTER = D // 4

COL_Q, COL_K, COL_V, COL_G = 0, 1024, 2048, 4096
COL_LR = 6144
COL_RX = COL_LR + RANK
COL_RY = COL_RX + D
COL_GA = COL_RY + D
COL_GB = COL_GA + D

PIECE = 1024
RING = 4
SLOTS = 8
GROUP = 256
N_RX, N_LG, N_HEAD, N_B, N_A, N_OUT, N_FFN, N_DOWN = 4, 1, 16, 8, 8, 4, FF // GROUP, FF // P // 4
I_RX = 0
I_LG = I_RX + N_RX
I_HEAD = I_LG + N_LG
I_B = I_HEAD + N_HEAD
I_A = I_B + N_B
I_OUT = I_A + N_A
I_FFN = I_OUT + N_OUT
I_DOWN = I_FFN + N_FFN
ITERS = I_DOWN + N_DOWN
G_RX = 0
G_B = G_RX + 2 * N_RX
G_A = G_B + 2 * N_B
G_FFN = G_A + 2 * N_A
G_END = G_FFN + 2 * N_FFN

PAR = {}
_at = 0
for _name, _n in (("conv_w", CONV * KT), ("conv_b", KT), ("b_a", KT), ("b_x", KT), ("lambda", KT),
                  ("b_alpha", HEADS * DK // P), ("norm_g", DV // P), ("ln1_g", KT), ("ln1_b", KT)):
    PAR[_name] = _at
    _at += _n
N_PAR = _at

FREE = 1
ACT_FREE = 2

LOG1P_TERMS = 9


class Steps:

    def __init__(self, eng, sem, trip=0, per=0):
        self.eng, self.sem, self.base, self.n, self.per = eng, sem, trip * per, 0, per

    def step(self, instruction):
        instruction.then_inc(self.sem, 1)
        self.n += 1

    def wait(self):
        self.eng.wait_ge(self.sem, self.base + self.n)

    def end(self):
        assert self.n == self.per, (self.n, self.per)


def build(nc, x, w_in, w_alpha, w_o, lru_w, rnn_o, w_out, w_gu, w_down, params, ln1_g, ln1_b, ln2_g, ln2_b, out):
    with ExitStack() as ctx:
        def sb(name, shape, dt=F32, stack=ctx):
            return stack.enter_context(nc.sbuf_tensor(name, shape, dt))

        def sem(name):
            return ctx.enter_context(nc.semaphore(name))

        raw = sb("raw", [P, RING, PIECE])
        w_hi = sb("w_hi", [P, RING, PIECE], F32R)
        w_lo = sb("w_lo", [P, RING, PIECE], F32R)
        x_t = sb("x_t", [P, KT, 2 * T], F32R)
        par = sb("par", [P, N_PAR])
        ident = sb("ident", [P, P])
        corr = sb("corr", [P, 4, T])
        one_col = sb("one_col", [P, 1])
        scratch = sb("scratch", [P, 2])
        gsum = sb("gsum", [P, 2, T])
        psum = ctx.enter_context(nc.psum_tensor("psum", [P, 8, 2 * T], F32))

        with ExitStack() as st:
            lr_raw = sb("lr_raw", [P, KT, RANK], stack=st)
            lr_hi = sb("lr_hi", [P, KT, P], F32R, stack=st)
            lr_lo = sb("lr_lo", [P, KT, P], F32R, stack=st)
            x_in = sb("x_in", [P, TT, D], stack=st)
        with ExitStack() as st:
            gates = sb("gates", [P, KT, 2 * T], stack=st)
        with ExitStack() as st:
            h_ff = sb("h_ff", [P, FF // P, T], stack=st)
            tok_g1 = sb("tok_g1", [P, D], stack=st)
            tok_b1 = sb("tok_b1", [P, D], stack=st)
        o_t = sb("o_t", [P, KT, 2 * T], F32R)
        b_t = sb("b_t", [P, KT, 2 * T], F32R)
        with ExitStack() as st:
            merged = sb("merged", [P, KT, T], stack=st)
            yb = sb("yb", [P, 2, T], stack=st)
            stage = sb("stage", [P, 4, 2 * T], F32R, stack=st)
            res = sb("res", [P, TT, D], stack=st)
            ln_t = sb("ln_t", [P, 4, 4, P], stack=st)
            stats = sb("stats", [P, TT, 4, 6], stack=st)
            mv = sb("mv", [P, TT, 4], stack=st)
        with ExitStack() as st:
            rx_pad = sb("rx_pad", [P, 2, 2, T + CONV - 1], stack=st)
            conv_y = sb("conv_y", [P, 2, T], stack=st)
        v_h = sb("v_h", [P, TT, DV])
        state = sb("state", [P, 2, DV])
        alpha_cur = sb("alpha_cur", [RANK, DK])
        lr_t = sb("lr_t", [RANK, T])
        lru_c = sb("lru_c", [P, KT])
        lamt = sb("lamt", [P, 4, KT])
        o_sq = sb("o_sq", [P, TT, 4, P])
        lru_a = sb("lru_a", [P, 4, T])
        lru_m = sb("lru_m", [P, 4, T])
        h_lru = sb("h_lru", [P, 4, T])
        ones_dv = sb("ones_dv", [P, P])
        chunk_mask = sb("chunk_mask", [P, 2 * T], BF16)
        bc = sb("bc", [P, 2, T])
        e_pos = sb("e_pos", [P, 2, T])
        e_neg = sb("e_neg", [P, 2, T])
        qk_dec = sb("qk_dec", [P, 2, 2, T])
        k_end = sb("k_end", [P, 2, T])
        k_end_t = sb("k_end_t", [P, TT, DK])
        scores = sb("scores", [P, TT, CHUNK])
        silu_g = sb("silu_g", [P, 4, T])
        rstd = sb("rstd", [P, TT, P])
        y_act = corr[:, :, :]
        a_sq = o_sq[:, :, :, :].rearrange("p t (a b) i -> p (t a) (b i)", b=2)
        o_g = qk_dec[:, :, :, :].rearrange("p a b t -> p (a b) t")

        raw_landed = [sem(f"raw_landed{s}") for s in range(RING)]
        hi_ready, lo_ready, piece_done = sem("hi_ready"), sem("lo_ready"), sem("piece_done")
        corr_out, group_read = sem("corr_out"), sem("group_read")
        x_landed = [sem(f"x_landed{c}") for c in range(4)]
        par_landed, lrw_landed, alpha_landed = sem("par_landed"), sem("lrw_landed"), sem("alpha_landed")
        consts, x_turned, x_hi_out, x_lo_out = sem("consts"), sem("x_turned"), sem("x_hi_out"), sem("x_lo_out")
        lr_hi_ready, lr_lo_ready, lr_done, lr_ready, lr_set = (
            sem("lr_hi_ready"), sem("lr_lo_ready"), sem("lr_done"), sem("lr_ready"), sem("lr_set"))
        lam_exp = sem("lam_exp")
        dve_pro, dve_rx, dve_head, dve_ln = sem("dve_pro"), sem("dve_rx"), sem("dve_head"), sem("dve_ln")
        lam_pre = sem("lam_pre")
        conv_out, conv_hi, conv_lo = sem("conv_out"), sem("conv_hi"), sem("conv_lo")
        tap0 = sem("tap0")
        lg_read = sem("lg_read")
        alpha_done, alpha_out, ls_exp, ls_ln, bc_ready = (
            sem("alpha_done"), sem("alpha_out"), sem("ls_exp"), sem("ls_ln"), sem("bc_ready"))
        x_conv, ix_ready = sem("x_conv"), sem("ix_ready")
        decay_exp, decay_sq, h_ready = sem("decay_exp"), sem("decay_sq"), sem("h_ready")
        e_pos_ready, e_neg_ready, k_diff, e_end_ready, dec_ready = (
            sem("e_pos_ready"), sem("e_neg_ready"), sem("k_diff"), sem("e_end_ready"), sem("dec_ready"))
        kt_done, kt_out, sc_out, sc_masked = sem("kt_done"), sem("kt_out"), sem("sc_out"), sem("sc_masked")
        v_out, chunk_done, state_ready, o_done = sem("v_out"), sem("chunk_done"), sem("state_ready"), sem("o_done")
        sq_ready, ms_done, og_ready, og_hi, og_lo = (
            sem("sq_ready"), sem("ms_done"), sem("og_ready"), sem("og_hi"), sem("og_lo"))
        act_ready, b_ready, b_hi, b_lo = sem("act_ready"), sem("b_ready"), sem("b_hi"), sem("b_lo")
        gated, merged_ready, ff_ready = sem("gated"), sem("merged_ready"), sem("ff_ready")
        stage_hi, stage_ready = sem("stage_hi"), sem("stage_ready")
        res_landed, tok_landed, z_ready, mv_ready, z_norm = (
            sem("res_landed"), sem("tok_landed"), sem("z_ready"), sem("mv_ready"), sem("z_norm"))
        tile0_done = sem("tile0_done")
        ln_turned, ln_out, ln_hi, ln_lo = ([sem(f"{n}{tt}") for tt in range(TT)]
                                           for n in ("ln_turned", "ln_out", "ln_hi", "ln_lo"))
        pool_res, res_step, ln2_landed = sem("pool_res"), sem("res_step"), sem("ln2_landed")
        scaled, out_ready, out_ready_pool, stored = sem("scaled"), sem("out_ready"), sem("out_ready_pool"), sem("stored")
        gap_ready, gap_root, rms_inv, rms_root = sem("gap_ready"), sem("gap_root"), sem("rms_inv"), sem("rms_root")
        table_ready = sem("table_ready")
        ln_inv, ln_root = sem("ln_inv"), sem("ln_root")
        pool_set, mask_ready = sem("pool_set"), sem("mask_ready")

        def pcol(name, i, n=1):
            return par[:, bass.ds(PAR[name] + i, n)]

        block = ctx.enter_context(nc.Block())

        @block.sync
        def _(sp):
            w_in_v = w_in.rearrange("(k p) c -> p k c", p=P)
            for c in range(4):
                sp.dma_start(x_in[:, :, c * 512:(c + 1) * 512],
                             x[:, c * 512:(c + 1) * 512].rearrange("(t p) d -> p t d", p=P)).then_inc(x_landed[c], 16)
            sp.dma_start(par[:, :], params).then_inc(par_landed, 16)

            def load(it, p, source, first=False):
                if not first:
                    sp.wait_ge(lo_ready, SLOTS * it + p - RING + 1)
                s = p % RING
                dst = raw[:, s, :]
                if len(source.shape) == 3:
                    dst = dst.rearrange("p (k c) -> p k c", k=source.shape[1])
                sp.dma_start(dst, source).then_inc(raw_landed[s], 16)

            def columns(w, it, half, col, first=False):
                for q in range(4):
                    load(it, 4 * half + q, w[:, 4 * q:4 * q + 4, bass.ds(col, GROUP)], first)

            rx = lambda j, half: COL_RX + 2 * GROUP * j + GROUP * half
            columns(w_in_v, 0, 0, rx(0, 0), first=True)
            columns(w_in_v, 0, 1, rx(0, 1))
            sp.dma_start(lr_raw[:, :, :], w_in_v[:, :, COL_LR:COL_LR + RANK]).then_inc(lrw_landed, 16)
            with sp.Fori(1, N_RX) as j:
                columns(w_in_v, j + I_RX, 0, rx(j, 0))
                columns(w_in_v, j + I_RX, 1, rx(j, 1))
            for p in range(SLOTS):
                load(I_LG, p, lru_w[p])
            w_v = w_in.rearrange("(q k p) c -> q p k c", p=P, k=2)
            with sp.Fori(0, HEADS) as j:
                it = 4 * j + I_HEAD
                columns(w_in_v, it, 0, COL_Q + DK * j)
                columns(w_in_v, it, 1, COL_K + DK * j)
                for p in range(SLOTS):
                    load(it + 1, p, w_v[p, :, :, bass.ds(COL_V + DV * j, DV)])
                columns(w_in_v, it + 2, 0, COL_G + DV * j)
                columns(w_in_v, it + 2, 1, COL_G + DV * j + GROUP)
                columns(w_in_v, it + 3, 0, COL_RY + 2 * GROUP * j)
                columns(w_in_v, it + 3, 1, COL_RY + 2 * GROUP * j + GROUP)
            for base, n, w, col in ((I_B, N_B, rnn_o, COL_GB), (I_A, N_A, w_o, COL_GA)):
                w = w.rearrange("(k p) c -> p k c", p=P)
                with sp.Fori(base, base + n) as it:
                    columns(w_in_v, it, 0, GROUP * it + (col - GROUP * base))
                    columns(w, it, 1, GROUP * it - GROUP * base)
            w_rows = w_out.rearrange("(k p) (h c) -> k h p c", p=P, c=PIECE)
            with sp.Fori(0, N_OUT) as j:
                for p in range(SLOTS):
                    load(j + I_OUT, p, w_rows[bass.ds(4 * j + p // 2, 1), p % 2].rearrange("a p c -> (a p) c"))
            w_gu_v = w_gu.rearrange("(k p) c -> p k c", p=P)
            with sp.Fori(0, N_FFN) as j:
                columns(w_gu_v, j + I_FFN, 0, GROUP * j)
                columns(w_gu_v, j + I_FFN, 1, FF + GROUP * j)
            w_rows2 = w_down.rearrange("(k p) (h c) -> k h p c", p=P, c=PIECE)
            with sp.Fori(0, N_DOWN) as j:
                for p in range(SLOTS):
                    load(j + I_DOWN, p, w_rows2[bass.ds(4 * j + p // 2, 1), p % 2].rearrange("a p c -> (a p) c"))
            sp.wait_ge(pool_res, TT)
            sp.dma_start(tok_g1[:, :], ln2_g.to_broadcast([P, D])).then_inc(ln2_landed, 16)
            sp.dma_start(tok_b1[:, :], ln2_b.to_broadcast([P, D])).then_inc(ln2_landed, 16)
            for tt, b in ((0, 0), (0, 1), (1, 0), (0, 2), (1, 1), (1, 2), (0, 3), (1, 3)):
                sp.wait_ge((out_ready_pool, out_ready)[tt], b + 1)
                part = slice(b * QUARTER, (b + 1) * QUARTER)
                sp.dma_start(out[tt * P:(tt + 1) * P, part], res[:, tt, part]).then_inc(stored, 16)
            sp.wait_ge(stored, 16 * 4 * TT)

        @block.tensor
        def _(pe):
            def mm(o, w, m, start, stop):
                return nc.tensor.matmul(o, w, m, start=start, stop=stop)

            def arrived(it, p):
                pe.wait_ge(lo_ready, SLOTS * it + p + 1)

            def tile_product(bank, hi, lo, moving, first, last):
                whole, main = psum[:, bank, :], psum[:, bank, 0:T]
                if first:
                    mm(whole, hi, moving, True, False)
                    return mm(main, lo, moving[:, 0:T], False, False)
                mm(main, lo, moving[:, 0:T], False, False)
                return mm(whole, hi, moving, False, last)

            def narrow_product(bank, hi, lo, moving, first, last):
                main = psum[:, bank, 0:T]
                mm(main, hi, moving[:, 0:T], first, False)
                mm(main, hi, moving[:, T:2 * T], False, False)
                return mm(main, lo, moving[:, 0:T], False, last)

            def piece(it, p, moving, banks, product):
                arrived(it, p)
                s, q = p % RING, p % 4
                for i in range(4):
                    for c in range(2):
                        w = slice(i * GROUP + c * P, i * GROUP + (c + 1) * P)
                        last = product(banks + c, w_hi[:, s, w], w_lo[:, s, w], moving[:, 4 * q + i, :],
                                       q == 0 and i == 0, q == 3 and i == 3)
                last.then_inc(piece_done, 1)

            def group(it, half, moving, g, after=(), product=tile_product):
                if g is not None:
                    pe.wait_ge(group_read, g - 1)
                for q in range(4):
                    piece(it, 4 * half + q, moving, 2 * half, product)
                    if q < len(after) and after[q]:
                        after[q]()

            def token_tile(p, at, act, banks, n_of, first, last, tiles=range(TT)):
                s = p % RING
                for tt in tiles:
                    hi, lo = act[:, tt * P:(tt + 1) * P], act[:, T + tt * P:T + (tt + 1) * P]
                    for n in range(n_of):
                        bank = banks(tt, n)
                        m = slice(at + n * 512, at + (n + 1) * 512)
                        mm(psum[:, bank, :], hi, w_hi[:, s, m], first, False)
                        mm(psum[:, bank, :], hi, w_lo[:, s, m], False, False)
                        r = mm(psum[:, bank, :], lo, w_hi[:, s, m], False, last)
                return r

            pe.sem_inc(ms_done, FREE)
            pe.sem_inc(act_ready, ACT_FREE)
            pe.wait_ge(consts, 2)
            for q in range(KT // 2):
                if q % 2 == 0:
                    pe.wait_ge(x_landed[q // 2], 16)
                for k in range(2):
                    for tt in range(TT):
                        at = k * T + tt * P
                        r = nc.tensor.transpose(psum[:, q, at:at + P],
                                                x_in[:, tt, (2 * q + k) * P:(2 * q + k + 1) * P], ident[:, :])
                r.then_inc(x_turned, 1)

            for q in range(4):
                pe.wait_ge(x_lo_out, 2 * q + 2)
                piece(0, q, x_t, 0, narrow_product)
            group(0, 1, x_t, None, product=narrow_product)
            with pe.Fori(1, N_RX) as j:
                group(j + I_RX, 0, x_t, 2 * j + G_RX, product=narrow_product)
                group(j + I_RX, 1, x_t, 2 * j + G_RX + 1, product=narrow_product)

            pe.wait_ge(lr_lo_ready, 1)
            for kt in range(KT):
                r = narrow_product(4, lr_hi[:, kt, :], lr_lo[:, kt, :], x_t[:, kt, :], kt == 0, kt == KT - 1)
            r.then_inc(lr_done, 1)

            for p in range(SLOTS):
                arrived(I_LG, p)
                s, base = p % RING, 4 * (p % 2)
                if p == 0:
                    pe.wait_ge(group_read, G_B)
                if p == 1:
                    pe.wait_ge(lr_ready, 1)
                if p >= 2:
                    pe.wait_ge(lg_read, p - 1)
                pe.wait_ge(conv_lo, FREE + p + 1)
                for kt in range(2):
                    for g in range(4):
                        w = slice(kt * 512 + g * P, kt * 512 + (g + 1) * P)
                        last = narrow_product(base + g, w_hi[:, s, w], w_lo[:, s, w], b_t[:, 2 * p + kt, :],
                                              kt == 0, kt == 1)
                last.then_inc(piece_done, 1)
            pe.wait_ge(lg_read, SLOTS)

            with pe.Fori(0, HEADS) as j:
                it = 4 * j + I_HEAD

                def alpha():
                    pe.wait_ge(alpha_landed, 16 * j + 16)
                    pe.wait_ge(o_done, FREE + 2 * j)
                    for c in range(2):
                        r = mm(psum[:, 4, c * T:(c + 1) * T], alpha_cur[:, c * P:(c + 1) * P], lr_t[:, :], True, True)
                    r.then_inc(alpha_done, 1)

                def keys_and_scores():
                    pe.wait_ge(dec_ready, FREE + 3 * j + 3)
                    pe.wait_ge(alpha_out, j + 1)
                    for tt in range(TT):
                        for c in range(2):
                            nc.tensor.transpose(psum[:, 4, tt * DK + c * P:tt * DK + (c + 1) * P],
                                                k_end[:, c, tt * P:(tt + 1) * P], ident[:, :])
                    for n in range(NCHUNK):
                        tt, at = n // 2, CHUNK * (n % 2)
                        tok = slice(n * CHUNK, (n + 1) * CHUNK)
                        for c in range(2):
                            r = mm(psum[at:at + CHUNK, 5, tt * CHUNK:(tt + 1) * CHUNK], qk_dec[:, 1, c, tok],
                                   qk_dec[:, 0, c, tok], c == 0, c == 1)
                    r.then_inc(kt_done, 1)

                def chunk(n):
                    tt, at = n // 2, CHUNK * (n % 2)
                    rows, tok = slice(at, at + CHUNK), slice(n * CHUNK, (n + 1) * CHUNK)
                    if n == 0:
                        pe.wait_ge(kt_out, j + 1)
                        pe.wait_ge(sc_masked, 2 * j + 2)
                        pe.wait_ge(v_out, j + 1)
                    else:
                        pe.wait_ge(state_ready, FREE + 3 * j + n)
                    for b in range(DV // P):
                        o = psum[:, 4 + tt, b * P + at:b * P + at + CHUNK]
                        dv = slice(b * P, (b + 1) * P)
                        if n:
                            mm(o, state[:, 0, dv], qk_dec[:, 0, 0, tok], True, False)
                            mm(o, state[:, 1, dv], qk_dec[:, 0, 1, tok], False, False)
                        r = mm(o, v_h[rows, tt, dv], scores[rows, tt, :], n == 0, True)
                    if n < NCHUNK - 1:
                        for c in range(2):
                            r = mm(psum[:, 6 + c, :], k_end_t[rows, tt, c * P:(c + 1) * P], v_h[rows, tt, :], True, True)
                    r.then_inc(chunk_done, 1)

                def mean_square():
                    pe.wait_ge(sq_ready, j + 1)
                    for b in range(DV // P):
                        r = mm(psum[:, 6, 0:T].rearrange("p (t i) -> p t i", t=TT), ones_dv[:, :], o_sq[:, :, b, :],
                               b == 0, b == DV // P - 1)
                    r.then_inc(ms_done, 1)

                pe.wait_ge(act_ready, ACT_FREE + 4 * j - 1)
                group(it, 0, x_t, None, (alpha,), narrow_product)
                pe.wait_ge(act_ready, ACT_FREE + 4 * j)
                group(it, 1, x_t, None, (), narrow_product)
                for p in range(SLOTS):
                    arrived(it + 1, p)
                    if p == 0:
                        pe.wait_ge(og_ready, FREE + 2 * j)
                    for i in range(2):
                        r = token_tile(p, i * DV, x_t[:, 2 * p + i, :], lambda tt, n: 6 + tt, 1,
                                       p == 0 and i == 0, p == SLOTS - 1 and i == 1)
                    r.then_inc(piece_done, 1)
                    if p == 4:
                        keys_and_scores()
                group(it + 2, 0, x_t, None, (None, lambda: chunk(0), None, lambda: chunk(1)), narrow_product)
                group(it + 2, 1, x_t, None, (None, lambda: chunk(2), None, lambda: chunk(3)), narrow_product)
                pe.wait_ge(act_ready, ACT_FREE + 4 * j + 1)
                group(it + 3, 0, x_t, None, (None, mean_square), narrow_product)
                pe.wait_ge(act_ready, ACT_FREE + 4 * j + 2)
                group(it + 3, 1, x_t, None, (), narrow_product)

            pe.wait_ge(act_ready, ACT_FREE + 4 * HEADS - 1)
            for base, gb, n, act in ((I_B, G_B, N_B, b_t), (I_A, G_A, N_A, o_t)):
                with pe.Fori(0, n) as j:
                    group(j + base, 0, x_t, 2 * j + gb)
                    pe.wait_ge(b_lo, FREE + 2 * HEADS)
                    group(j + base, 1, act, 2 * j + gb + 1)

            def token_piece(it, p, first=False, last=False, tiles=range(TT)):
                return token_tile(p, 0, stage[:, p // 2, :], lambda tt, n: 4 * tt + 2 * (p % 2) + n, 2,
                                  first, last, tiles)

            def token_major(it, done, pieces=range(SLOTS), first_it=False, groups=0):
                for p in pieces:
                    arrived(it, p)
                    if p % 2 == 0:
                        pe.wait_ge(stage_ready, done + p // 2 + 1)
                    if first_it and p == 0:
                        pe.wait_ge(group_read, groups - 1)
                    if first_it and p == 1:
                        pe.wait_ge(group_read, groups)
                    token_piece(it, p, first_it and p < 2).then_inc(piece_done, 1)

            def last_token_major(it, done):
                token_major(it, done, range(SLOTS - RING))
                for tt in range(TT):
                    for p in range(SLOTS - RING, SLOTS):
                        if tt == 0:
                            arrived(it, p)
                            if p % 2 == 0:
                                pe.wait_ge(stage_ready, done + p // 2 + 1)
                        r = token_piece(it, p, False, p >= SLOTS - 2, (tt,))
                        if tt == 1:
                            r.then_inc(piece_done, 1)
                        elif p >= SLOTS - 2:
                            r.then_inc(tile0_done, 1)

            token_major(I_OUT, 0, first_it=True, groups=G_FFN)
            with pe.Fori(1, N_OUT - 1) as j:
                token_major(j + I_OUT, 4 * j)
            last_token_major(I_OUT + N_OUT - 1, 4 * (N_OUT - 1))

            for tt in range(TT):
                for b in range(4):
                    pe.wait_ge(z_norm, 4 * tt + b + 1)
                    for i in range(4):
                        kt = 4 * b + i
                        r = nc.tensor.transpose(psum[:, 4 * tt + b, i * P:(i + 1) * P],
                                                res[:, tt, kt * P:(kt + 1) * P], ident[:, :])
                    r.then_inc(ln_turned[tt], 1)
            for q in range(4):
                for tt in range(TT):
                    pe.wait_ge(ln_lo[tt], q + 1)
                piece(I_FFN, q, x_t, 0, tile_product)
            group(I_FFN, 1, x_t, None)
            with pe.Fori(1, N_FFN) as j:
                group(j + I_FFN, 0, x_t, 2 * j + G_FFN)
                group(j + I_FFN, 1, x_t, 2 * j + G_FFN + 1)
            token_major(I_DOWN, 4 * N_OUT, first_it=True, groups=G_END)
            with pe.Fori(1, N_DOWN - 1) as j:
                token_major(j + I_DOWN, 4 * j + 4 * N_OUT)
            last_token_major(I_DOWN + N_DOWN - 1, 4 * (N_OUT + N_DOWN - 1))

        @block.scalar
        def _(act):
            A = nc.scalar.activation

            def split(it, p, ahead=RING):
                s = p % RING
                if ahead:
                    act.wait_ge(piece_done, SLOTS * it + p + 1)
                act.wait_ge(raw_landed[s], 32 * it + 16 * ((p + ahead) // RING + 1))
                A(w_hi[:, s, :], raw[:, s, :], ACT.Copy).then_inc(hi_ready, 1)

            def copy_corr(half):
                A(corr[:, 2 * half:2 * half + 2, :], psum[:, 2 * half:2 * half + 2, T:2 * T], ACT.Copy)\
                    .then_inc(corr_out, 1)

            for q in range(KT // 2):
                act.wait_ge(x_turned, q + 1)
                A(x_t[:, 2 * q:2 * q + 2, 0:T], psum[:, q, :].rearrange("p (k t) -> p k t", k=2), ACT.Copy)\
                    .then_inc(x_hi_out, 1)
                if q >= 5:
                    split(0, q - 5, 0)
            split(0, 3, 0)
            act.wait_ge(lam_pre, 1)
            A(lamt[:, 1, :], lamt[:, 0, :], ACT.Exp, scale=-1.0).then_inc(lam_exp, 1)

            act.wait_ge(lrw_landed, 16)
            act.wait_ge(lr_set, 2)
            A(lr_hi[:, :, 0:RANK], lr_raw[:, :, :], ACT.Copy).then_inc(lr_hi_ready, 1)
            act.wait_ge(dve_pro, 2)
            with act.Fori(0, N_RX) as j:
                for p in range(SLOTS):
                    split(j + I_RX, p)
                    if p % 4 == 3:
                        half = p // 4
                        act.wait_ge(conv_lo, FREE + 2 * j + half)
                        A(rx_pad[:, half, :, CONV - 1:], psum[:, 2 * half:2 * half + 2, 0:T], ACT.Copy)\
                            .then_inc(group_read, 1)
                        act.wait_ge(group_read, 2 * j + half + 1)
                        for c in range(2):
                            t = 4 * j + 2 * half + c
                            r = A(conv_y[:, c, :], rx_pad[:, half, c, 0:T], ACT.Identity,
                                  bias=pcol("conv_b", t), scale=pcol("conv_w", t))
                            r.then_inc(tap0, 1)
                    if p in (5, 7):
                        half = p // 7
                        act.wait_ge(conv_out, 2 * j + half + 1)
                        A(b_t[:, bass.ds(4 * j + 2 * half, 2), 0:T], conv_y[:, :, :], ACT.Copy).then_inc(conv_hi, 1)

            act.wait_ge(lr_done, 1)
            A(lr_t[:, :], psum[0:RANK, 4, 0:T], ACT.Copy).then_inc(lr_ready, 1)
            for p in range(SLOTS):
                split(I_LG, p)
                for g, name in enumerate(("b_a", "b_x")):
                    for c in range(2):
                        t = 2 * p + c
                        r = A(gates[:, t, g * T:(g + 1) * T], psum[:, 4 * (p % 2) + 2 * g + c, 0:T], ACT.Sigmoid,
                              bias=pcol(name, t))
                r.then_inc(lg_read, 1)

            with act.Fori(0, HEADS) as j:
                it = 4 * j + I_HEAD

                def decays(m):
                    if m == 0:
                        act.wait_ge(h_ready, FREE + j)
                        act.wait_ge(lg_read, SLOTS)
                    for f, to in ((ACT.Exp, lru_a), (ACT.Tanh, lru_m)):
                        for c in (2 * m, 2 * m + 1):
                            t = bass.ds(4 * j + c, 1)
                            A(to[:, c, :], gates[:, t, 0:T].rearrange("p a t -> p (a t)"), f, scale=lru_c[:, t])\
                                .then_inc(decay_exp, 1)

                for p in range(SLOTS):
                    split(it, p)
                    if p < 2:
                        decays(p)
                    if p == 4:
                        act.wait_ge(ms_done, FREE + j)
                        act.wait_ge(decay_exp, 8 * j + 8)
                        A(a_sq, lru_a[:, :, :], ACT.Square).then_inc(decay_sq, 1)
                    if p == 2:
                        act.wait_ge(alpha_out, j + 1)
                        A(e_neg[:, :, :], e_neg[:, :, :], ACT.Exp, scale=-1.0).then_inc(ls_exp, 1)
                    if p == 6:
                        act.wait_ge(ls_exp, j + 1)
                        A(e_neg[:, :, :], e_neg[:, :, :], ACT.Ln, bias=one_col[:, 0:1]).then_inc(ls_ln, 1)
                for p in range(SLOTS):
                    if p == 0:
                        act.wait_ge(bc_ready, j + 1)
                        A(e_pos[:, :, :], bc[:, :, :], ACT.Exp, scale=1.0 / TAU).then_inc(e_pos_ready, 1)
                        A(e_neg[:, :, :], bc[:, :, :], ACT.Exp, scale=-1.0 / TAU).then_inc(e_neg_ready, 1)
                    if p == 1:
                        act.wait_ge(k_diff, FREE + j + 1)
                        A(k_end[:, :, :], k_end[:, :, :], ACT.Exp, scale=-1.0 / TAU).then_inc(e_end_ready, 1)
                    if p == 3:
                        act.wait_ge(gap_ready, j + 1)
                        A(lru_m[:, :, :], lru_m[:, :, :], ACT.Sqrt, scale=-1.0).then_inc(gap_root, 1)
                    split(it + 1, p)
                    if p == 6:
                        act.wait_ge(kt_done, j + 1)
                        A(scores[:, :, :], psum[:, 5, 0:2 * CHUNK].rearrange("p (t i) -> p t i", t=TT), ACT.Copy)\
                            .then_inc(sc_out, 1)
                        A(k_end_t[:, :, :], psum[:, 4, :].rearrange("p (t c) -> p t c", t=TT), ACT.Copy)\
                            .then_inc(kt_out, 1)
                    if p == 7:
                        A(v_h[:, :, :], psum[:, 6:8, :], ACT.Copy).then_inc(v_out, 1)
                for p in range(SLOTS):
                    split(it + 2, p)
                    if p % 4 == 3:
                        two = slice(2 * (p // 4), 2 * (p // 4) + 2)
                        if p == 3:
                            act.wait_ge(og_ready, FREE + 2 * j)
                        A(silu_g[:, two, :], psum[:, two, 0:T], ACT.Silu).then_inc(act_ready, 1)
                for p in range(SLOTS):
                    if p == 6:
                        act.wait_ge(og_ready, FREE + 2 * j + 2)
                    split(it + 3, p)
                    if p == 0:
                        act.wait_ge(chunk_done, 4 * j + 4)
                        act.wait_ge(h_ready, FREE + j + 1)
                        A(o_sq[:, :, :, :], psum[:, 4:6, :].rearrange("p t (b i) -> p t b i", b=4), ACT.Square).then_inc(sq_ready, 1)
                    if p == 2:
                        act.wait_ge(rms_inv, j + 1)
                        A(rstd[:, :, :], rstd[:, :, :], ACT.Sqrt).then_inc(rms_root, 1)
                    if p == 6:
                        A(o_t[:, bass.ds(4 * j, 4), 0:T], o_g, ACT.Copy).then_inc(og_hi, 1)
                    if p % 4 == 3:
                        two = slice(2 * (p // 4), 2 * (p // 4) + 2)
                        if p == 3:
                            act.wait_ge(b_lo, FREE + 2 * j)
                        A(y_act[:, two, :], psum[:, two, 0:T], ACT.Gelu_apprx_tanh).then_inc(act_ready, 1)
                    if p in (4, 7):
                        half = p // 7
                        act.wait_ge(b_ready, FREE + 2 * j + half + 1)
                        A(b_t[:, bass.ds(4 * j + 2 * half, 2), 0:T], y_act[:, 2 * half:2 * half + 2, :], ACT.Copy)\
                            .then_inc(b_hi, 1)

            def stage_tile(m, source):
                A(stage[:, m, 0:T], source, ACT.Copy).then_inc(stage_hi, 1)

            act.wait_ge(b_lo, FREE + 2 * HEADS)
            A(scratch[:, 0:1], one_col[:, :], ACT.Sigmoid).then_inc(table_ready, 1)

            def merge_iteration(j, k, base, then_stage=False):
                for p in range(SLOTS):
                    split(j + base, p)
                    if p == 3:
                        copy_corr(0)
                        act.wait_ge(group_read, 2 * j + G_B + 2 * k * N_B + 1)
                        A(gsum[:, :, :], gsum[:, :, :], ACT.Sigmoid).then_inc(act_ready, 1)
                    if p == 5 and then_stage:
                        act.wait_ge(merged_ready, FREE + N_B + 2)
                        for m in range(4):
                            stage_tile(m, merged[:, m, :])
                    if p == 7:
                        copy_corr(1)

            with act.Fori(0, N_B) as j:
                merge_iteration(j, 0, I_B)
            with act.Fori(0, N_A - 1) as j:
                merge_iteration(j, 1, I_A)
            merge_iteration(N_A - 1, 1, I_A, then_stage=True)
            act.wait_ge(piece_done, SLOTS * I_OUT)
            act.dma_start(res[:, :, :], x.rearrange("(t p) d -> p t d", p=P)).then_inc(res_landed, 16)
            act.dma_start(tok_g1[:, :], ln1_g.to_broadcast([P, D])).then_inc(tok_landed, 16)
            act.dma_start(tok_b1[:, :], ln1_b.to_broadcast([P, D])).then_inc(tok_landed, 16)
            def token_major(it, j, source, last_it):
                for p in range(SLOTS):
                    if not (last_it and p >= SLOTS - RING and source is h_ff):
                        split(it, p)
                    if p % 2 == 1 and not last_it:
                        m = p // 2
                        act.wait_ge(piece_done, SLOTS * it + p + 1)
                        stage_tile(m, source[:, bass.ds(4 * j + 4 + m, 1), :].rearrange("p a t -> p (a t)"))

            act.wait_ge(merged_ready, FREE + 2 * N_B)
            with act.Fori(0, N_OUT - 1) as j:
                token_major(j + I_OUT, j, merged, False)
            token_major(I_OUT + N_OUT - 1, 0, merged, True)

            def normalise(tt, ln):
                act.wait_ge(ln_inv, TT * ln + tt + 1)
                A(mv[:, tt, 2:3], mv[:, tt, 2:3], ACT.Sqrt).then_inc(ln_root, 1)
                act.wait_ge(mv_ready, TT * ln + tt + 1)
                for b in range(4):
                    z = res[:, tt, b * QUARTER:(b + 1) * QUARTER]
                    A(z, z, ACT.Identity, bias=mv[:, tt, 3:4], scale=mv[:, tt, 2:3]).then_inc(z_norm, 1)

            def ln_hi_part(tt, b):
                A(x_t[:, 4 * b:4 * b + 4, tt * P:(tt + 1) * P], ln_t[:, b, :, :], ACT.Copy).then_inc(ln_hi[tt], 1)

            def tile0_channels(b):
                act.wait_ge(ln_turned[0], b + 1)
                for i in range(4):
                    r = A(ln_t[:, b, i, :], psum[:, b, i * P:(i + 1) * P], ACT.Identity, bias=pcol("ln1_b", 4 * b + i),
                          scale=pcol("ln1_g", 4 * b + i))
                r.then_inc(ln_out[0], 1)
                act.wait_ge(ln_out[0], b + 1)
                ln_hi_part(0, b)

            def tile1_hi(b):
                act.wait_ge(ln_out[1], b + 1)
                ln_hi_part(1, b)

            normalise(0, 0)
            tile0_channels(0)
            tile0_channels(1)
            normalise(1, 0)
            tile1_hi(0)
            tile0_channels(2)
            tile1_hi(1)
            tile0_channels(3)
            tile1_hi(2)
            tile1_hi(3)

            A(scratch[:, 1:2], scratch[:, 0:1], ACT.Silu).then_inc(table_ready, 1)

            def ffn_iteration(j, then_stage=False):
                for p in range(SLOTS):
                    split(j + I_FFN, p)
                    if p == 3:
                        copy_corr(0)
                        act.wait_ge(group_read, 2 * j + G_FFN + 1)
                        act.wait_ge(ff_ready, FREE + j)
                        A(yb[:, :, :], gsum[:, :, :], ACT.Silu).then_inc(act_ready, 1)
                    if p == 5 and then_stage:
                        act.wait_ge(ff_ready, FREE + 2)
                        for m in range(4):
                            stage_tile(m, h_ff[:, m, :])
                    if p == 7:
                        copy_corr(1)

            with act.Fori(0, N_FFN - 1) as j:
                ffn_iteration(j)
            ffn_iteration(N_FFN - 1, then_stage=True)
            act.wait_ge(ff_ready, FREE + N_FFN)
            with act.Fori(0, N_DOWN - 1) as j:
                token_major(j + I_DOWN, j, h_ff, False)
            token_major(I_DOWN + N_DOWN - 1, 0, h_ff, True)
            for tt in range(TT):
                normalise(tt, 1)

        @block.vector
        def _(dve):
            tt_op, ts_op, stt = nc.vector.tensor_tensor, nc.vector.tensor_scalar, nc.vector.scalar_tensor_tensor

            def split(it, p, ahead=RING):
                s = p % RING
                dve.wait_ge(hi_ready, SLOTS * it + p + ahead + 1)
                tt_op(w_lo[:, s, :], raw[:, s, :], w_hi[:, s, :].bitcast(F32), ALU.subtract).then_inc(lo_ready, 1)

            def group_sum(to, half, g):
                dve.wait_ge(corr_out, g - G_B + 1)
                tt_op(to, psum[:, 2 * half:2 * half + 2, 0:T], corr[:, 2 * half:2 * half + 2, :], ALU.add)\
                    .then_inc(group_read, 1)

            for free in (state_ready, dec_ready, k_diff, o_done, og_ready, h_ready, b_lo, conv_lo, merged_ready,
                         ff_ready, og_lo, b_ready):
                dve.sem_inc(free, FREE)
            pro = Steps(dve, dve_pro)
            pro.step(nc.vector.memset(rx_pad[:, :, :, 0:CONV - 1], 0.0))
            pro.step(nc.vector.memset(one_col[:, :], 1.0))
            for q in range(KT // 2):
                dve.wait_ge(x_hi_out, q + 1)
                tt_op(x_t[:, 2 * q:2 * q + 2, T:2 * T], psum[:, q, :].rearrange("p (k t) -> p k t", k=2),
                      x_t[:, 2 * q:2 * q + 2, 0:T].bitcast(F32), ALU.subtract).then_inc(x_lo_out, 1)
                if q >= 5:
                    split(0, q - 5, 0)
            split(0, 3, 0)
            dve.wait_ge(par_landed, 16)
            lam = pcol("lambda", 0, KT)
            stt(lamt[:, 0, :], lam, -1.0, lam, ALU.mult, ALU.max).then_inc(lam_pre, 1)

            dve.wait_ge(lr_hi_ready, 1)
            tt_op(lr_lo[:, :, 0:RANK], lr_raw[:, :, :], lr_hi[:, :, 0:RANK].bitcast(F32), ALU.subtract).then_inc(lr_lo_ready, 1)
            per = 2 * 2 * (CONV - 2)
            with dve.Fori(0, N_RX) as j:
                own = Steps(dve, dve_rx, j, per)
                for p in range(SLOTS):
                    split(j + I_RX, p)
                    if p % 4 == 3:
                        half = p // 4
                        b = 2 * j + half
                        for k in range(1, CONV):
                            if k == 1:
                                dve.wait_ge(tap0, 2 * b + 2)
                            else:
                                own.wait()
                            for c in range(2):
                                w = par[:, bass.ds(4 * j + PAR["conv_w"] + k * KT + 2 * half + c, 1)]
                                r = stt(conv_y[:, c, :], rx_pad[:, half, c, k:k + T], w, conv_y[:, c, :],
                                        ALU.mult, ALU.add)
                                if k < CONV - 1:
                                    own.step(r)
                        r.then_inc(conv_out, 1)
                        dve.wait_ge(conv_hi, b + 1)
                        tile = bass.ds(4 * j + 2 * half, 2)
                        tt_op(b_t[:, tile, T:2 * T], conv_y[:, :, :], b_t[:, tile, 0:T].bitcast(F32), ALU.subtract)\
                            .then_inc(conv_lo, 1)
                own.end()

            def lru_decay_scale():
                dve.wait_ge(lam_exp, 1)
                y, s_, z_, acc = lamt[:, 1, :], lamt[:, 2, :], lamt[:, 3, :], lru_c[:, :]
                pro.step(ts_op(s_, y, 2.0, None, ALU.add))
                pro.wait()
                pro.step(nc.vector.reciprocal(s_, s_))
                pro.wait()
                pro.step(tt_op(s_, s_, y, ALU.mult))
                pro.wait()
                pro.step(tt_op(z_, s_, s_, ALU.mult))
                pro.step(nc.vector.memset(acc, 1.0 / (2 * LOG1P_TERMS - 1)))
                for n in range(LOG1P_TERMS - 2, -1, -1):
                    pro.wait()
                    pro.step(tt_op(acc, acc, z_, ALU.mult))
                    pro.wait()
                    pro.step(ts_op(acc, acc, 1.0 / (2 * n + 1), None, ALU.add))
                pro.wait()
                pro.step(tt_op(acc, acc, s_, ALU.mult))
                pro.step(ts_op(y, lam, -1.0, 0.0, ALU.mult, ALU.max))
                pro.wait()
                pro.step(ts_op(y, y, -LRU_C, None, ALU.mult))
                pro.wait()
                pro.step(stt(acc, acc, -2.0 * LRU_C, y, ALU.mult, ALU.add))
                pro.wait()

            for p in range(SLOTS):
                split(I_LG, p)
                if p == 2:
                    lru_decay_scale()

            per = 2 + 1 + 1 + 1
            with dve.Fori(0, HEADS) as j:
                it = 4 * j + I_HEAD
                own = Steps(dve, dve_head, j, per)

                def lru_scan():
                    dve.wait_ge(gap_root, j + 1)
                    dve.wait_ge(b_ready, FREE + 2 * j)
                    dve.wait_ge(ix_ready, SLOTS)
                    own.step(tt_op(h_lru[:, :, :], gates[:, bass.ds(4 * j, 4), T:2 * T], lru_m[:, :, :], ALU.mult))
                    own.wait()
                    for c in range(4):
                        r = nc.vector.tensor_tensor_scan(h_lru[:, c, :], lru_a[:, c, :], h_lru[:, c, :], 0.0,
                                                         ALU.mult, ALU.add)
                    r.then_inc(h_ready, 1)

                for p in range(SLOTS):
                    split(it, p)
                    if p == 1:
                        dve.wait_ge(alpha_done, j + 1)
                        dve.wait_ge(state_ready, FREE + 3 * j)
                        dve.wait_ge(dec_ready, FREE + 3 * j)
                        for c in range(2):
                            own.step(ts_op(e_pos[:, c, :], psum[:, 4, c * T:(c + 1) * T], pcol("b_alpha", 2 * j + c), None,
                                           ALU.add))
                        own.wait()
                        stt(e_neg[:, :, :], e_pos[:, :, :], -1.0, e_pos[:, :, :], ALU.mult, ALU.max).then_inc(alpha_out, 1)
                    if p == 5:
                        dve.wait_ge(decay_sq, j + 1)
                        stt(lru_m[:, :, :], a_sq, 1.0, lru_m[:, :, :], ALU.add, ALU.mult).then_inc(gap_ready, 1)
                    if p == 7:
                        dve.wait_ge(ls_ln, j + 1)
                        own.step(stt(e_pos[:, :, :], e_pos[:, :, :], 0.0, e_neg[:, :, :], ALU.min, ALU.subtract))
                        own.wait()
                        dve.wait_ge(mask_ready, 1)
                        dve.wait_ge(k_diff, FREE + j)
                        nc.vector.tensor_tensor_scan(bc[:, :, :].rearrange("p c t -> p (c t)"), chunk_mask[:, :],
                                                     e_pos[:, :, :].rearrange("p c t -> p (c t)"), 0.0,
                                                     ALU.mult, ALU.add).then_inc(bc_ready, 1)
                        dve.wait_ge(bc_ready, j + 1)
                        v = lambda t: t[:, :, :].rearrange("p c (n t) -> p (c n) t", t=CHUNK)
                        tt_op(v(k_end), v(bc), v(bc)[:, :, CHUNK - 1:CHUNK].to_broadcast([P, 2 * NCHUNK, CHUNK]),
                              ALU.subtract).then_inc(k_diff, 1)
                for p in range(SLOTS):
                    split(it + 1, p)
                    if p == 1:
                        dve.wait_ge(e_pos_ready, j + 1)
                        dve.wait_ge(piece_done, SLOTS * it + SLOTS)
                        dve.wait_ge(og_lo, FREE + j)
                        stt(qk_dec[:, 0, :, :], psum[:, 0:2, 0:T], DK ** -0.5, e_pos[:, :, :], ALU.mult, ALU.mult)\
                            .then_inc(dec_ready, 1)
                        dve.wait_ge(e_neg_ready, j + 1)
                        tt_op(qk_dec[:, 1, :, :], psum[:, 2:4, 0:T], e_neg[:, :, :], ALU.mult).then_inc(dec_ready, 1)
                    if p == 2:
                        dve.wait_ge(e_end_ready, j + 1)
                        tt_op(k_end[:, :, :], psum[:, 2:4, 0:T], k_end[:, :, :], ALU.mult).then_inc(dec_ready, 1)
                    if p == 4:
                        lru_scan()
                for p in range(SLOTS):
                    if p in (2, 4, 6):
                        n = p // 2 - 1
                        dve.wait_ge(chunk_done, 4 * j + n + 1)
                        dve.wait_ge(state_ready, FREE + 3 * j + n)
                        for c in range(2):
                            if n == 0:
                                r = nc.vector.tensor_copy(state[:, c, :], psum[:, 6 + c, :])
                            else:
                                at = n * CHUNK + CHUNK - 1
                                r = stt(state[:, c, :], state[:, c, :], e_pos[:, c, at:at + 1], psum[:, 6 + c, :],
                                        ALU.mult, ALU.add)
                        r.then_inc(state_ready, 1)
                    split(it + 2, p)
                for p in range(SLOTS):
                    split(it + 3, p)
                    if p == 2:
                        dve.wait_ge(ms_done, FREE + j + 1)
                        own.step(ts_op(rstd[:, :, :], psum[:, 6, 0:T].rearrange("p (t i) -> p t i", t=TT), EPS, None,
                                       ALU.add))
                        own.wait()
                        nc.vector.reciprocal(rstd[:, :, :], rstd[:, :, :]).then_inc(rms_inv, 1)
                    if p == 4:
                        dve.wait_ge(rms_root, j + 1)
                        for tt in range(TT):
                            r = tt_op(o_g[:, :, tt * P:(tt + 1) * P], psum[:, 4 + tt, :].rearrange("p (b i) -> p b i", b=4),
                                      rstd[:, tt:tt + 1, :].to_broadcast([P, 4, P]), ALU.mult)
                            r.then_inc(o_done, 1)
                        dve.wait_ge(o_done, FREE + 2 * j + 2)
                        dve.wait_ge(act_ready, ACT_FREE + 4 * j + 2)
                        for b in range(4):
                            r = stt(o_g[:, b, :], o_g[:, b, :], pcol("norm_g", b), silu_g[:, b, :], ALU.mult, ALU.mult)
                            if b % 2:
                                r.then_inc(og_ready, 1)
                    if p % 4 == 3:
                        half = p // 4
                        y = y_act[:, 2 * half:2 * half + 2, :]
                        dve.wait_ge(act_ready, ACT_FREE + 4 * j + 3 + half)
                        dve.wait_ge(h_ready, FREE + j + 1)
                        tt_op(y, y, h_lru[:, 2 * half:2 * half + 2, :], ALU.mult).then_inc(b_ready, 1)
                        dve.wait_ge(b_hi, 2 * j + half + 1)
                        tile = bass.ds(4 * j + 2 * half, 2)
                        tt_op(b_t[:, tile, T:2 * T], y, b_t[:, tile, 0:T].bitcast(F32), ALU.subtract)\
                            .then_inc(b_lo, 1)
                    if p == 7:
                        dve.wait_ge(og_hi, j + 1)
                        tile = bass.ds(4 * j, 4)
                        tt_op(o_t[:, tile, T:2 * T], o_g, o_t[:, tile, 0:T].bitcast(F32), ALU.subtract)\
                            .then_inc(og_lo, 1)
                own.end()

            def stage_tile(n, m, source):
                dve.wait_ge(stage_hi, n + 1)
                tt_op(stage[:, m, T:2 * T], source, stage[:, m, 0:T].bitcast(F32), ALU.subtract)\
                    .then_inc(stage_ready, 1)

            def merge_iteration(j, k, base, then_stage=False):
                gb = G_B + 2 * k * N_B
                for p in range(SLOTS):
                    split(j + base, p)
                    if p == 3:
                        dve.wait_ge(merged_ready, FREE + j + k * N_B)
                        group_sum(gsum[:, :, :], 0, 2 * j + gb)
                    if p == 5 and then_stage:
                        for m in range(4):
                            stage_tile(m, m, merged[:, m, :])
                    if p == 7:
                        group_sum(yb[:, :, :], 1, 2 * j + gb + 1)
                        dve.wait_ge(group_read, 2 * j + gb + 2)
                        dve.wait_ge(act_ready, ACT_FREE + j + 4 * HEADS + k * N_B + 1)
                        to = merged[:, bass.ds(2 * j, 2), :]
                        if k == 0:
                            tt_op(to, gsum[:, :, :], yb[:, :, :], ALU.mult).then_inc(merged_ready, 1)
                        else:
                            tt_op(yb[:, :, :], gsum[:, :, :], yb[:, :, :], ALU.mult).then_inc(gated, 1)
                            dve.wait_ge(gated, j + 1)
                            tt_op(to, to, yb[:, :, :], ALU.add).then_inc(merged_ready, 1)

            with dve.Fori(0, N_B) as j:
                merge_iteration(j, 0, I_B)
            with dve.Fori(0, N_A - 1) as j:
                merge_iteration(j, 1, I_A)
            merge_iteration(N_A - 1, 1, I_A, then_stage=True)

            def token_major(it, j, first_tile, source, last_it=False):
                for p in range(SLOTS - RING if last_it else SLOTS):
                    split(it, p)
                    if p % 2 == 1 and not last_it:
                        m = p // 2
                        stage_tile(4 * j + 4 + m + first_tile, m,
                                   source[:, bass.ds(4 * j + 4 + m, 1), :].rearrange("p a t -> p (a t)"))

            def norm_stats(n, tt, end):
                own = Steps(dve, dve_ln)
                own.n = n
                for b in range(4):
                    if tt == 0:
                        dve.wait_ge(tile0_done, (0 if end == I_FFN else 2) + b // 2 + 1)
                    else:
                        dve.wait_ge(piece_done, SLOTS * end - 1 + b // 2)
                    z = res[:, tt, b * 512:(b + 1) * 512]
                    if end == I_FFN:
                        own.step(stt(z, z, ALPHA, psum[:, 4 * tt + b, :], ALU.mult, ALU.add))
                    else:
                        own.step(tt_op(z, z, psum[:, 4 * tt + b, :], ALU.add))
                    own.wait()
                    own.step(nc.vector.bn_stats(stats[:, tt, b, :], z))
                own.wait()
                own.step(nc.vector.bn_aggr(mv[:, tt, 0:2], stats[:, tt, :, :].rearrange("p b s -> p (b s)")))
                own.wait()
                own.step(ts_op(mv[:, tt, 2:3], mv[:, tt, 1:2], EPS, None, ALU.add))
                own.wait()
                nc.vector.reciprocal(mv[:, tt, 2:3], mv[:, tt, 2:3]).then_inc(ln_inv, 1)
                dve.wait_ge(ln_root, (0 if end == I_FFN else TT) + tt + 1)
                stt(mv[:, tt, 3:4], mv[:, tt, 0:1], -1.0, mv[:, tt, 2:3], ALU.mult, ALU.mult).then_inc(mv_ready, 1)
                return own.n

            dve.wait_ge(merged_ready, FREE + 2 * N_B)
            with dve.Fori(0, N_OUT - 1) as j:
                token_major(j + I_OUT, j, 0, merged)
            token_major(I_OUT + N_OUT - 1, 0, 0, merged, last_it=True)

            dve.wait_ge(res_landed, 16)
            n_ln = norm_stats(0, 0, I_FFN)
            n_ln = norm_stats(n_ln, 1, I_FFN)

            def ln_lo_part(tt, b):
                dve.wait_ge(ln_hi[tt], b + 1)
                tt_op(x_t[:, 4 * b:4 * b + 4, T + tt * P:T + (tt + 1) * P], ln_t[:, b, :, :],
                      x_t[:, 4 * b:4 * b + 4, tt * P:(tt + 1) * P].bitcast(F32), ALU.subtract).then_inc(ln_lo[tt], 1)

            split(I_FFN - 1, SLOTS - RING)
            ln_lo_part(0, 0)
            for b in range(4):
                dve.wait_ge(ln_turned[1], b + 1)
                dve.wait_ge(ln_lo[0], b + 1)
                for i in range(4):
                    r = ts_op(ln_t[:, b, i, :], psum[:, 4 + b, i * P:(i + 1) * P], pcol("ln1_g", 4 * b + i),
                              pcol("ln1_b", 4 * b + i), ALU.mult, ALU.add)
                r.then_inc(ln_out[1], 1)
                if b < 3:
                    split(I_FFN - 1, SLOTS - RING + b + 1)
                    ln_lo_part(0, b + 1)
                ln_lo_part(1, b)

            def ffn_iteration(j, then_stage=False):
                for p in range(SLOTS):
                    split(j + I_FFN, p)
                    if p == 3:
                        dve.wait_ge(ff_ready, FREE + j)
                        group_sum(gsum[:, :, :], 0, 2 * j + G_FFN)
                    if p == 5 and then_stage:
                        for m in range(4):
                            stage_tile(4 * N_OUT + m, m, h_ff[:, m, :])
                    if p == 7:
                        dve.wait_ge(act_ready, ACT_FREE + j + 4 * HEADS + 2 * N_B + 1)
                        group_sum(gsum[:, :, :], 1, 2 * j + G_FFN + 1)
                        dve.wait_ge(group_read, 2 * j + G_FFN + 2)
                        tt_op(h_ff[:, bass.ds(2 * j, 2), :], gsum[:, :, :], yb[:, :, :], ALU.mult)\
                            .then_inc(ff_ready, 1)

            with dve.Fori(0, N_FFN - 1) as j:
                ffn_iteration(j)
            ffn_iteration(N_FFN - 1, then_stage=True)
            dve.wait_ge(ff_ready, FREE + N_FFN)
            with dve.Fori(0, N_DOWN - 1) as j:
                token_major(j + I_DOWN, j, 4 * N_OUT, h_ff)
            token_major(I_DOWN + N_DOWN - 1, 0, 0, h_ff, last_it=True)

            dve.wait_ge(pool_res, TT)
            dve.wait_ge(mv_ready, TT)
            n_ln = norm_stats(n_ln, 0, ITERS)
            n_ln = norm_stats(n_ln, 1, ITERS)
            dve.wait_ge(ln2_landed, 32)
            for b in range(4):
                part = slice(b * QUARTER, (b + 1) * QUARTER)
                dve.wait_ge(z_norm, 4 * TT + 4 + b + 1)
                o = res[:, 1, part]
                tt_op(o, o, tok_g1[:, part], ALU.mult).then_inc(scaled, 1)
                dve.wait_ge(scaled, b + 1)
                tt_op(o, o, tok_b1[:, part], ALU.add).then_inc(out_ready, 1)

        @block.gpsimd
        def _(pool):
            pool.memset(ident[:, :], 0.0).then_inc(pool_set, 1)
            pool.memset(ones_dv[:, :], 1.0 / DV).then_inc(consts, 1)
            pool.memset(chunk_mask[:, :], 1.0).then_inc(pool_set, 1)
            for t in (lr_hi, lr_lo):
                pool.memset(t[:, :, RANK:P].bitcast(F32), 0.0).then_inc(lr_set, 1)
            pool.wait_ge(pool_set, 2)
            pool.affine_select(out=ident[:, :], in_=ident[:, :], compare_op=ALU.not_equal, fill=1.0, base=0,
                               pattern=[[-1, P]], channel_multiplier=1).then_inc(consts, 1)
            pool.memset(chunk_mask[:, :].rearrange("p (n t) -> p n t", t=CHUNK)[:, :, 0:1], 0.0).then_inc(mask_ready, 1)
            for p in range(SLOTS):
                two, part = slice(2 * p, 2 * p + 2), slice(2 * (p % 2), 2 * (p % 2) + 2)
                pool.wait_ge(conv_lo, FREE + p + 1)
                if p > 0:
                    pool.wait_ge(ix_ready, p)
                pool.tensor_tensor(h_lru[:, part, :], b_t[:, two, 0:T].bitcast(F32), b_t[:, two, T:2 * T].bitcast(F32),
                                   ALU.add).then_inc(x_conv, 1)
                pool.wait_ge(x_conv, p + 1)
                pool.wait_ge(lg_read, p + 1)
                pool.tensor_tensor(gates[:, two, T:2 * T], gates[:, two, T:2 * T], h_lru[:, part, :], ALU.mult)\
                    .then_inc(ix_ready, 1)
            pool.wait_ge(ix_ready, SLOTS)
            for j in range(HEADS):
                if j > 0:
                    pool.wait_ge(alpha_done, j)
                pool.dma_start(alpha_cur[:, :], w_alpha[:, DK * j:DK * (j + 1)]).then_inc(alpha_landed, 16)
                pool.wait_ge(sc_out, j + 1)
                for half in range(2):
                    s = scores[CHUNK * half:CHUNK * (half + 1), :, :]
                    pool.affine_select(out=s, in_=s, compare_op=ALU.is_ge, fill=0.0, base=0,
                                       pattern=[[0, TT], [1, CHUNK]], channel_multiplier=-1).then_inc(sc_masked, 1)
            pool.wait_ge(tok_landed, 32)
            for tt in range(TT):
                pool.wait_ge(ln_turned[tt], 4)
                z = res[:, tt, :]
                pool.tensor_tensor(z, z, tok_g1[:, :], ALU.mult).then_inc(res_step, 1)
                pool.wait_ge(res_step, 2 * tt + 1)
                pool.tensor_tensor(z, z, tok_b1[:, :], ALU.add).then_inc(res_step, 1)
                pool.wait_ge(res_step, 2 * tt + 2)
                pool.tensor_scalar(z, z, ALPHA, None, ALU.mult).then_inc(pool_res, 1)
            pool.wait_ge(ln2_landed, 32)
            for b in range(4):
                part = slice(b * QUARTER, (b + 1) * QUARTER)
                pool.wait_ge(z_norm, 4 * TT + b + 1)
                o = res[:, 0, part]
                pool.tensor_tensor(o, o, tok_g1[:, part], ALU.mult).then_inc(res_step, 1)
                pool.wait_ge(res_step, 2 * TT + b + 1)
                pool.tensor_tensor(o, o, tok_b1[:, part], ALU.add).then_inc(out_ready_pool, 1)


def kernel(x, w_in, gla_w_alpha, gla_b_alpha, gla_norm_g, gla_w_o, conv_w, conv_b, lru_w_a, lru_b_a, lru_w_x, lru_b_x,
           lru_lambda, rnn_w_o, w_out, ln1_g, ln1_b, w_gate_up, w_down, ln2_g, ln2_b):
    import concourse.bacc as bacc
    from concourse.bass_utils import run_bass_kernel_spmd

    def tiles(a):
        return np.asarray(a).reshape(-1, P).T

    params = np.concatenate([tiles(a) for a in (conv_w, conv_b, lru_b_a, lru_b_x, lru_lambda, gla_b_alpha,
                                                gla_norm_g, ln1_g, ln1_b)], axis=1)
    lru_w = np.stack([np.asarray(a)[0].reshape(8, 2, P, DK) for a in (lru_w_a, lru_w_x)], axis=3)
    lru_w = lru_w.transpose(0, 2, 1, 3, 4).reshape(8, P, PIECE)
    arrays = {
        "x": np.asarray(x)[0], "w_in": np.asarray(w_in)[0], "w_alpha": np.asarray(gla_w_alpha)[0],
        "w_o": np.asarray(gla_w_o)[0], "lru_w": lru_w, "rnn_o": np.asarray(rnn_w_o)[0],
        "w_out": np.asarray(w_out)[0], "w_gu": np.asarray(w_gate_up)[0], "w_down": np.asarray(w_down)[0],
        "params": params, "ln1_g": np.asarray(ln1_g), "ln1_b": np.asarray(ln1_b),
        "ln2_g": np.asarray(ln2_g), "ln2_b": np.asarray(ln2_b),
    }
    nc = bacc.Bacc("TRN2", target_bir_lowering=False, num_devices=1)
    arrays = {k: np.ascontiguousarray(a) for k, a in arrays.items()}
    aps = {k: nc.dram_tensor(k, a.shape, mybir.dt.from_np(a.dtype), kind="ExternalInput").ap()
           for k, a in arrays.items()}
    out = nc.dram_tensor("out", (T, D), F32, kind="ExternalOutput").ap()
    build(nc, out=out, **aps)
    r = run_bass_kernel_spmd(nc, [arrays], core_ids=[0])
    return r.results[0]["out"].reshape(1, T, D)
```

```python
from contextlib import ExitStack

import numpy as np

import concourse.bass as bass
from concourse import mybir

F32 = mybir.dt.float32
F32R = mybir.dt.float32r
BF16 = mybir.dt.bfloat16
ALU = mybir.AluOpType
ACT = mybir.ActivationFunctionType

P = 128
D = 2048
T = 256
TT = T // P
KT = D // P
HEADS = 4
DK = 256
DV = 512
CHUNK = 64
NCHUNK = T // CHUNK
RANK = 16
TAU = 16.0
LRU_C = 8.0
CONV = 4
FF = 5632
ALPHA = 2 ** 0.25
EPS = 1e-5
QUARTER = D // 4

COL_Q, COL_K, COL_V, COL_G = 0, 1024, 2048, 4096
COL_LR = 6144
COL_RX = COL_LR + RANK
COL_RY = COL_RX + D
COL_GA = COL_RY + D
COL_GB = COL_GA + D

PIECE = 1024
RING = 4
SLOTS = 8
GROUP = 256
N_RX, N_LG, N_HEAD, N_B, N_A, N_OUT, N_FFN, N_DOWN = 4, 1, 16, 8, 8, 4, FF // GROUP, FF // P // 4
I_RX = 0
I_LG = I_RX + N_RX
I_HEAD = I_LG + N_LG
I_B = I_HEAD + N_HEAD
I_A = I_B + N_B
I_OUT = I_A + N_A
I_FFN = I_OUT + N_OUT
I_DOWN = I_FFN + N_FFN
ITERS = I_DOWN + N_DOWN
G_RX = 0
G_B = G_RX + 2 * N_RX
G_A = G_B + 2 * N_B
G_FFN = G_A + 2 * N_A
G_END = G_FFN + 2 * N_FFN

PAR = {}
_at = 0
for _name, _n in (("conv_w", CONV * KT), ("conv_b", KT), ("b_a", KT), ("b_x", KT), ("lambda", KT),
                  ("b_alpha", HEADS * DK // P), ("norm_g", DV // P), ("ln1_g", KT), ("ln1_b", KT)):
    PAR[_name] = _at
    _at += _n
N_PAR = _at

FREE = 1
ACT_FREE = 2

LOG1P_TERMS = 9


class Steps:

    def __init__(self, eng, sem, trip=0, per=0):
        self.eng, self.sem, self.base, self.n, self.per = eng, sem, trip * per, 0, per

    def step(self, instruction):
        instruction.then_inc(self.sem, 1)
        self.n += 1

    def wait(self):
        self.eng.wait_ge(self.sem, self.base + self.n)

    def end(self):
        assert self.n == self.per, (self.n, self.per)


def build(nc, x, w_in, w_alpha, w_o, lru_w, rnn_o, w_out, w_gu, w_down, params, ln1_g, ln1_b, ln2_g, ln2_b, out):
    with ExitStack() as ctx:
        def sb(name, shape, dt=F32, stack=ctx):
            return stack.enter_context(nc.sbuf_tensor(name, shape, dt))

        def sem(name):
            return ctx.enter_context(nc.semaphore(name))

        raw = sb("raw", [P, RING, PIECE])
        w_hi = sb("w_hi", [P, RING, PIECE], F32R)
        w_lo = sb("w_lo", [P, RING, PIECE], F32R)
        x_t = sb("x_t", [P, KT, 2 * T], F32R)
        par = sb("par", [P, N_PAR])
        ident = sb("ident", [P, P])
        corr = sb("corr", [P, 4, T])
        one_col = sb("one_col", [P, 1])
        scratch = sb("scratch", [P, 2])
        gsum = sb("gsum", [P, 2, T])
        psum = ctx.enter_context(nc.psum_tensor("psum", [P, 8, 2 * T], F32))

        with ExitStack() as st:
            lr_raw = sb("lr_raw", [P, KT, RANK], stack=st)
            lr_hi = sb("lr_hi", [P, KT, P], F32R, stack=st)
            lr_lo = sb("lr_lo", [P, KT, P], F32R, stack=st)
            x_in = sb("x_in", [P, TT, D], stack=st)
        with ExitStack() as st:
            gates = sb("gates", [P, KT, 2 * T], stack=st)
        with ExitStack() as st:
            h_ff = sb("h_ff", [P, FF // P, T], stack=st)
            tok_g1 = sb("tok_g1", [P, D], stack=st)
            tok_b1 = sb("tok_b1", [P, D], stack=st)
        o_t = sb("o_t", [P, KT, 2 * T], F32R)
        b_t = sb("b_t", [P, KT, 2 * T], F32R)
        with ExitStack() as st:
            merged = sb("merged", [P, KT, T], stack=st)
            yb = sb("yb", [P, 2, T], stack=st)
            stage = sb("stage", [P, 4, 2 * T], F32R, stack=st)
            res = sb("res", [P, TT, D], stack=st)
            ln_t = sb("ln_t", [P, 6, 4, P], stack=st)
            stats = sb("stats", [P, TT, 4, 6], stack=st)
            mv = sb("mv", [P, TT, 4], stack=st)
        with ExitStack() as st:
            rx_pad = sb("rx_pad", [P, 2, 2, T + CONV - 1], stack=st)
            conv_y = sb("conv_y", [P, 2, T], stack=st)
        v_h = sb("v_h", [P, TT, DV])
        state = sb("state", [P, 2, DV])
        alpha_cur = sb("alpha_cur", [RANK, DK])
        lr_t = sb("lr_t", [RANK, T])
        lru_c = sb("lru_c", [P, KT])
        lamt = sb("lamt", [P, 4, KT])
        o_sq = sb("o_sq", [P, TT, 4, P])
        lru_a = sb("lru_a", [P, 4, T])
        lru_m = sb("lru_m", [P, 4, T])
        h_lru = sb("h_lru", [P, 4, T])
        ones_dv = sb("ones_dv", [P, P])
        chunk_mask = sb("chunk_mask", [P, 2 * T], BF16)
        bc = sb("bc", [P, 2, T])
        e_pos = sb("e_pos", [P, 2, T])
        e_neg = sb("e_neg", [P, 2, T])
        qk_dec = sb("qk_dec", [P, 2, 2, T])
        k_end = sb("k_end", [P, 2, T])
        k_end_t = sb("k_end_t", [P, TT, DK])
        scores = sb("scores", [P, TT, P])
        silu_g = sb("silu_g", [P, 4, T])
        rstd = sb("rstd", [P, TT, P])
        y_act = corr[:, :, :]
        a_sq = o_sq[:, :, :, :].rearrange("p t (a b) i -> p (t a) (b i)", b=2)
        o_g = qk_dec[:, :, :, :].rearrange("p a b t -> p (a b) t")

        def ln_place(tt, b):
            return b if tt == 0 else (4 + b) % 6

        LN_BANK = ((0, 2, 3, 4), (1, 5, 6, 7))
        LN_STEPS = 11

        raw_landed = [sem(f"raw_landed{s}") for s in range(RING)]
        hi_ready, lo_ready, piece_done = sem("hi_ready"), sem("lo_ready"), sem("piece_done")
        corr_out, group_read = sem("corr_out"), sem("group_read")
        x_landed = [sem(f"x_landed{c}") for c in range(4)]
        par_landed, lrw_landed, alpha_landed = sem("par_landed"), sem("lrw_landed"), sem("alpha_landed")
        consts, x_turned, x_hi_out, x_lo_out = sem("consts"), sem("x_turned"), sem("x_hi_out"), sem("x_lo_out")
        lr_hi_ready, lr_lo_ready, lr_done, lr_ready, lr_set = (
            sem("lr_hi_ready"), sem("lr_lo_ready"), sem("lr_done"), sem("lr_ready"), sem("lr_set"))
        lam_exp = sem("lam_exp")
        dve_pro, dve_rx, dve_head, dve_ln = sem("dve_pro"), sem("dve_rx"), sem("dve_head"), sem("dve_ln")
        lam_pre = sem("lam_pre")
        conv_out, conv_hi, conv_lo = sem("conv_out"), sem("conv_hi"), sem("conv_lo")
        tap0 = sem("tap0")
        lg_read = sem("lg_read")
        alpha_done, alpha_out, ls_exp, ls_ln, bc_ready = (
            sem("alpha_done"), sem("alpha_out"), sem("ls_exp"), sem("ls_ln"), sem("bc_ready"))
        lru_c_ready, x_conv, ix_ready = sem("lru_c_ready"), sem("x_conv"), sem("ix_ready")
        decay_exp, decay_sq, h_ready = sem("decay_exp"), sem("decay_sq"), sem("h_ready")
        e_pos_ready, e_neg_ready, k_diff, e_end_ready, dec_ready = (
            sem("e_pos_ready"), sem("e_neg_ready"), sem("k_diff"), sem("e_end_ready"), sem("dec_ready"))
        kt_done, kt_out, sc_out, sc_masked = sem("kt_done"), sem("kt_out"), sem("sc_out"), sem("sc_masked")
        v_out, chunk_done, state_ready, o_done = sem("v_out"), sem("chunk_done"), sem("state_ready"), sem("o_done")
        sq_ready, ms_done, og_ready, og_hi, og_lo = (
            sem("sq_ready"), sem("ms_done"), sem("og_ready"), sem("og_hi"), sem("og_lo"))
        act_ready, b_ready, b_hi, b_lo = sem("act_ready"), sem("b_ready"), sem("b_hi"), sem("b_lo")
        gated, merged_ready, ff_ready = sem("gated"), sem("merged_ready"), sem("ff_ready")
        stage_hi, stage_ready = sem("stage_hi"), sem("stage_ready")
        res_landed, tok_landed, z_norm = sem("res_landed"), sem("tok_landed"), sem("z_norm")
        sq_step, sq_sum = sem("sq_step"), sem("sq_sum")
        tile0_done, tile1_half = sem("tile0_done"), sem("tile1_half")
        ln_turned, ln_out, ln_hi, ln_lo = ([sem(f"{n}{tt}") for tt in range(TT)]
                                           for n in ("ln_turned", "ln_out", "ln_hi", "ln_lo"))
        pool_res, res_step, ln2_landed = sem("pool_res"), sem("res_step"), sem("ln2_landed")
        scaled, out_ready, out_ready_pool, stored = (
            sem("scaled"), sem("out_ready"), sem("out_ready_pool"), sem("stored"))
        gap_ready, gap_root, rms_inv, rms_root = sem("gap_ready"), sem("gap_root"), sem("rms_inv"), sem("rms_root")
        table_ready = sem("table_ready")
        ln_inv, ln_root = sem("ln_inv"), sem("ln_root")
        pool_set, mask_ready = sem("pool_set"), sem("mask_ready")

        def pcol(name, i, n=1):
            return par[:, bass.ds(PAR[name] + i, n)]

        block = ctx.enter_context(nc.Block())

        @block.sync
        def _(sp):
            w_in_v = w_in.rearrange("(k p) c -> p k c", p=P)

            def load(it, p, source, first=False):
                if not first:
                    sp.wait_ge(lo_ready, SLOTS * it + p - RING + 1)
                s = p % RING
                dst = raw[:, s, :]
                if len(source.shape) == 3:
                    dst = dst.rearrange("p (k c) -> p k c", k=source.shape[1])
                sp.dma_start(dst, source).then_inc(raw_landed[s], 16)

            def columns(w, it, half, col):
                for q in range(4):
                    load(it, 4 * half + q, w[:, 4 * q:4 * q + 4, bass.ds(col, GROUP)])

            rx = lambda j, half: COL_RX + 2 * GROUP * j + GROUP * half
            for c in range(4):
                sp.dma_start(x_in[:, :, c * 512:(c + 1) * 512],
                             x[:, c * 512:(c + 1) * 512].rearrange("(t p) d -> p t d", p=P)).then_inc(x_landed[c], 16)
                load(0, c, w_in_v[:, 4 * c:4 * c + 4, rx(0, 0):rx(0, 0) + GROUP], first=True)
            sp.dma_start(par[:, :], params).then_inc(par_landed, 16)
            sp.dma_start(lr_raw[:, :, :], w_in_v[:, :, COL_LR:COL_LR + RANK]).then_inc(lrw_landed, 16)
            columns(w_in_v, 0, 1, rx(0, 1))
            with sp.Fori(1, N_RX) as j:
                columns(w_in_v, j + I_RX, 0, rx(j, 0))
                columns(w_in_v, j + I_RX, 1, rx(j, 1))
            for p in range(SLOTS):
                load(I_LG, p, lru_w[p])
            w_v = w_in.rearrange("(q k p) c -> q p k c", p=P, k=2)
            with sp.Fori(0, HEADS) as j:
                it = 4 * j + I_HEAD
                columns(w_in_v, it, 0, COL_Q + DK * j)
                columns(w_in_v, it, 1, COL_K + DK * j)
                for p in range(SLOTS):
                    load(it + 1, p, w_v[p, :, :, bass.ds(COL_V + DV * j, DV)])
                columns(w_in_v, it + 2, 0, COL_G + DV * j)
                columns(w_in_v, it + 2, 1, COL_G + DV * j + GROUP)
                columns(w_in_v, it + 3, 0, COL_RY + 2 * GROUP * j)
                columns(w_in_v, it + 3, 1, COL_RY + 2 * GROUP * j + GROUP)
            for base, n, w, col in ((I_B, N_B, rnn_o, COL_GB), (I_A, N_A, w_o, COL_GA)):
                w = w.rearrange("(k p) c -> p k c", p=P)
                with sp.Fori(base, base + n) as it:
                    columns(w_in_v, it, 0, GROUP * it + (col - GROUP * base))
                    columns(w, it, 1, GROUP * it - GROUP * base)
            w_rows = w_out.rearrange("(k p) (h c) -> k h p c", p=P, c=PIECE)
            with sp.Fori(0, N_OUT) as j:
                for p in range(SLOTS):
                    load(j + I_OUT, p, w_rows[bass.ds(4 * j + p // 2, 1), p % 2].rearrange("a p c -> (a p) c"))
            w_gu_v = w_gu.rearrange("(k p) c -> p k c", p=P)
            with sp.Fori(0, N_FFN) as j:
                columns(w_gu_v, j + I_FFN, 0, GROUP * j)
                columns(w_gu_v, j + I_FFN, 1, FF + GROUP * j)
            w_rows2 = w_down.rearrange("(k p) (h c) -> k h p c", p=P, c=PIECE)
            with sp.Fori(0, N_DOWN) as j:
                for p in range(SLOTS):
                    load(j + I_DOWN, p, w_rows2[bass.ds(4 * j + p // 2, 1), p % 2].rearrange("a p c -> (a p) c"))
            sp.wait_ge(pool_res, TT)
            sp.dma_start(tok_g1[:, :], ln2_g.to_broadcast([P, D])).then_inc(ln2_landed, 16)
            sp.dma_start(tok_b1[:, :], ln2_b.to_broadcast([P, D])).then_inc(ln2_landed, 16)
            for tt, b in ((0, 0), (0, 1), (1, 0), (0, 2), (1, 1), (1, 2), (0, 3), (1, 3)):
                sp.wait_ge((out_ready_pool, out_ready)[tt], b + 1)
                part = slice(b * QUARTER, (b + 1) * QUARTER)
                sp.dma_start(out[tt * P:(tt + 1) * P, part], res[:, tt, part]).then_inc(stored, 16)
            sp.wait_ge(stored, 16 * 4 * TT)

        @block.tensor
        def _(pe):
            def mm(o, w, m, start, stop):
                return nc.tensor.matmul(o, w, m, start=start, stop=stop)

            def arrived(it, p):
                pe.wait_ge(lo_ready, SLOTS * it + p + 1)

            def tile_product(bank, hi, lo, moving, first, last):
                whole, main = psum[:, bank, :], psum[:, bank, 0:T]
                if first:
                    mm(whole, hi, moving, True, False)
                    return mm(main, lo, moving[:, 0:T], False, False)
                mm(main, lo, moving[:, 0:T], False, False)
                return mm(whole, hi, moving, False, last)

            def narrow_product(bank, hi, lo, moving, first, last):
                main = psum[:, bank, 0:T]
                mm(main, hi, moving[:, 0:T], first, False)
                mm(main, hi, moving[:, T:2 * T], False, False)
                return mm(main, lo, moving[:, 0:T], False, last)

            def piece(it, p, moving, banks, product):
                arrived(it, p)
                s, q = p % RING, p % 4
                for i in range(4):
                    for c in range(2):
                        w = slice(i * GROUP + c * P, i * GROUP + (c + 1) * P)
                        last = product(banks + c, w_hi[:, s, w], w_lo[:, s, w], moving[:, 4 * q + i, :],
                                       q == 0 and i == 0, q == 3 and i == 3)
                last.then_inc(piece_done, 1)

            def group(it, half, moving, g, after=(), product=tile_product):
                if g is not None:
                    pe.wait_ge(group_read, g - 1)
                for q in range(4):
                    piece(it, 4 * half + q, moving, 2 * half, product)
                    if q < len(after) and after[q]:
                        after[q]()

            def token_tile(p, at, act, banks, n_of, first, last, tiles=range(TT)):
                s = p % RING
                for tt in tiles:
                    hi, lo = act[:, tt * P:(tt + 1) * P], act[:, T + tt * P:T + (tt + 1) * P]
                    for n in range(n_of):
                        bank = banks(tt, n)
                        m = slice(at + n * 512, at + (n + 1) * 512)
                        mm(psum[:, bank, :], hi, w_hi[:, s, m], first, False)
                        mm(psum[:, bank, :], hi, w_lo[:, s, m], False, False)
                        r = mm(psum[:, bank, :], lo, w_hi[:, s, m], False, last)
                return r

            pe.sem_inc(ms_done, FREE)
            pe.sem_inc(act_ready, ACT_FREE)
            pe.wait_ge(consts, 2)
            def turn(q):
                if q % 2 == 0:
                    pe.wait_ge(x_landed[q // 2], 16)
                for k in range(2):
                    for tt in range(TT):
                        at = k * T + tt * P
                        r = nc.tensor.transpose(psum[:, q, at:at + P],
                                                x_in[:, tt, (2 * q + k) * P:(2 * q + k + 1) * P], ident[:, :])
                r.then_inc(x_turned, 1)

            turn(0)
            turn(1)
            for q in range(4):
                if q < 3:
                    turn(2 * q + 2)
                    turn(2 * q + 3)
                pe.wait_ge(x_lo_out, 2 * q + 2)
                piece(0, q, x_t, 0, narrow_product)
            pe.wait_ge(x_lo_out, KT // 2)
            group(0, 1, x_t, None, product=narrow_product)
            with pe.Fori(1, N_RX) as j:
                group(j + I_RX, 0, x_t, 2 * j + G_RX, product=narrow_product)
                group(j + I_RX, 1, x_t, 2 * j + G_RX + 1, product=narrow_product)

            pe.wait_ge(lr_lo_ready, 1)
            for kt in range(KT):
                r = narrow_product(4, lr_hi[:, kt, :], lr_lo[:, kt, :], x_t[:, kt, :], kt == 0, kt == KT - 1)
            r.then_inc(lr_done, 1)

            for p in range(SLOTS):
                arrived(I_LG, p)
                s, base = p % RING, 4 * (p % 2)
                if p == 0:
                    pe.wait_ge(group_read, G_B)
                if p == 1:
                    pe.wait_ge(lr_ready, 1)
                if p >= 2:
                    pe.wait_ge(lg_read, p - 1)
                pe.wait_ge(conv_lo, FREE + p + 1)
                for kt in range(2):
                    for g in range(4):
                        w = slice(kt * 512 + g * P, kt * 512 + (g + 1) * P)
                        last = narrow_product(base + g, w_hi[:, s, w], w_lo[:, s, w], b_t[:, 2 * p + kt, :],
                                              kt == 0, kt == 1)
                last.then_inc(piece_done, 1)
            pe.wait_ge(lg_read, SLOTS - 1)

            with pe.Fori(0, HEADS) as j:
                it = 4 * j + I_HEAD

                def alpha():
                    pe.wait_ge(alpha_landed, 16 * j + 16)
                    pe.wait_ge(lg_read, SLOTS)
                    pe.wait_ge(o_done, FREE + 2 * j)
                    for c in range(2):
                        r = mm(psum[:, 4, c * T:(c + 1) * T], alpha_cur[:, c * P:(c + 1) * P], lr_t[:, :], True, True)
                    r.then_inc(alpha_done, 1)

                def keys_and_scores():
                    pe.wait_ge(dec_ready, FREE + 3 * j + 3)
                    pe.wait_ge(alpha_out, j + 1)
                    for tt in range(TT):
                        for c in range(2):
                            nc.tensor.transpose(psum[:, 4, tt * DK + c * P:tt * DK + (c + 1) * P],
                                                k_end[:, c, tt * P:(tt + 1) * P], ident[:, :])
                    for tt in range(TT):
                        tok = slice(tt * P, (tt + 1) * P)
                        for c in range(2):
                            r = mm(psum[:, 5, tok], qk_dec[:, 1, c, tok], qk_dec[:, 0, c, tok], c == 0, c == 1)
                    r.then_inc(kt_done, 1)

                def chunk(n):
                    tt, at = n // 2, CHUNK * (n % 2)
                    rows, tok = slice(at, at + CHUNK), slice(n * CHUNK, (n + 1) * CHUNK)
                    if n == 0:
                        pe.wait_ge(kt_out, j + 1)
                        pe.wait_ge(sc_masked, j + 1)
                        pe.wait_ge(v_out, j + 1)
                    else:
                        pe.wait_ge(state_ready, FREE + 3 * j + n)
                    for b in range(DV // P):
                        dv = slice(b * P, (b + 1) * P)
                        if n % 2 == 0:
                            r = mm(psum[:, 4 + tt, dv], v_h[:, tt, dv], scores[:, tt, :], b == 0, False)
                        if n:
                            o = psum[:, 4 + tt, b * P + at:b * P + at + CHUNK]
                            mm(o, state[:, 0, dv], qk_dec[:, 0, 0, tok], False, False)
                            r = mm(o, state[:, 1, dv], qk_dec[:, 0, 1, tok], False, n % 2 == 1 and b == DV // P - 1)
                    if n < NCHUNK - 1:
                        for c in range(2):
                            r = mm(psum[:, 6 + c, :], k_end_t[rows, tt, c * P:(c + 1) * P], v_h[rows, tt, :],
                                   True, True)
                    r.then_inc(chunk_done, 1)

                def mean_square():
                    pe.wait_ge(sq_sum, j + 1)
                    r = mm(psum[:, 6, 0:T].rearrange("p (t i) -> p t i", t=TT), ones_dv[:, :], o_sq[:, :, 0, :],
                           True, True)
                    r.then_inc(ms_done, 1)

                pe.wait_ge(act_ready, ACT_FREE + 4 * j - 1)
                group(it, 0, x_t, None, (alpha,), narrow_product)
                pe.wait_ge(act_ready, ACT_FREE + 4 * j)
                group(it, 1, x_t, None, (), narrow_product)
                for p in range(SLOTS):
                    arrived(it + 1, p)
                    if p == 0:
                        pe.wait_ge(og_ready, FREE + 2 * j)
                    for i in range(2):
                        r = token_tile(p, i * DV, x_t[:, 2 * p + i, :], lambda tt, n: 6 + tt, 1,
                                       p == 0 and i == 0, p == SLOTS - 1 and i == 1)
                    r.then_inc(piece_done, 1)
                    if p == 4:
                        keys_and_scores()
                group(it + 2, 0, x_t, None, (None, lambda: chunk(0), None, lambda: chunk(1)), narrow_product)
                group(it + 2, 1, x_t, None, (None, lambda: chunk(2), None, lambda: chunk(3)), narrow_product)
                pe.wait_ge(act_ready, ACT_FREE + 4 * j + 1)
                group(it + 3, 0, x_t, None, (None, None, mean_square), narrow_product)
                pe.wait_ge(act_ready, ACT_FREE + 4 * j + 2)
                group(it + 3, 1, x_t, None, (), narrow_product)

            pe.wait_ge(act_ready, ACT_FREE + 4 * HEADS - 1)
            for base, gb, n, act in ((I_B, G_B, N_B, b_t), (I_A, G_A, N_A, o_t)):
                with pe.Fori(0, n) as j:
                    group(j + base, 0, x_t, 2 * j + gb)
                    pe.wait_ge(b_lo, FREE + 2 * HEADS)
                    group(j + base, 1, act, 2 * j + gb + 1)

            def token_piece(it, p, first=False, last=False, tiles=range(TT)):
                return token_tile(p, 0, stage[:, p // 2, :], lambda tt, n: 4 * tt + 2 * (p % 2) + n, 2,
                                  first, last, tiles)

            def token_major(it, done, pieces=range(SLOTS), first_it=False, groups=0):
                for p in pieces:
                    arrived(it, p)
                    if p % 2 == 0:
                        pe.wait_ge(stage_ready, done + p // 2 + 1)
                    if first_it and p == 0:
                        pe.wait_ge(group_read, groups - 1)
                    if first_it and p == 1:
                        pe.wait_ge(group_read, groups)
                    token_piece(it, p, first_it and p < 2).then_inc(piece_done, 1)

            def last_token_major(it, done):
                token_major(it, done, range(SLOTS - RING))
                order = (SLOTS - 4, SLOTS - 2, SLOTS - 3, SLOTS - 1)
                for tt in range(TT):
                    for p in order:
                        if tt == 0:
                            arrived(it, p)
                            pe.wait_ge(stage_ready, done + p // 2 + 1)
                        r = token_piece(it, p, False, p >= SLOTS - 2, (tt,))
                        if tt == 0 and p >= SLOTS - 2:
                            r.then_inc(tile0_done, 1)
                        elif tt == 1 and p == SLOTS - 2:
                            r.then_inc(tile1_half, 1)
                        elif tt == 1:
                            r.then_inc(piece_done, 2 if p == SLOTS - 1 else 1)

            token_major(I_OUT, 0, first_it=True, groups=G_FFN)
            with pe.Fori(1, N_OUT - 1) as j:
                token_major(j + I_OUT, 4 * j)
            last_token_major(I_OUT + N_OUT - 1, 4 * (N_OUT - 1))

            for tt in range(TT):
                for b in range(4):
                    pe.wait_ge(z_norm, 4 * tt + b + 1)
                    if LN_BANK[tt][b] >= 4 * tt + 4:
                        pe.wait_ge(dve_ln, LN_STEPS + 1)
                    for i in range(4):
                        kt = 4 * b + i
                        r = nc.tensor.transpose(psum[:, LN_BANK[tt][b], i * P:(i + 1) * P],
                                                res[:, tt, kt * P:(kt + 1) * P], ident[:, :])
                    r.then_inc(ln_turned[tt], 1)
            for q in range(4):
                for tt in range(TT):
                    pe.wait_ge(ln_lo[tt], q + 1)
                piece(I_FFN, q, x_t, 0, tile_product)
            group(I_FFN, 1, x_t, None)
            with pe.Fori(1, N_FFN) as j:
                group(j + I_FFN, 0, x_t, 2 * j + G_FFN)
                group(j + I_FFN, 1, x_t, 2 * j + G_FFN + 1)
            token_major(I_DOWN, 4 * N_OUT, first_it=True, groups=G_END)
            with pe.Fori(1, N_DOWN - 1) as j:
                token_major(j + I_DOWN, 4 * j + 4 * N_OUT)
            last_token_major(I_DOWN + N_DOWN - 1, 4 * (N_OUT + N_DOWN - 1))

        @block.scalar
        def _(act):
            A = nc.scalar.activation

            def split(it, p, ahead=RING):
                s = p % RING
                if ahead:
                    act.wait_ge(piece_done, SLOTS * it + p + 1)
                act.wait_ge(raw_landed[s], 32 * it + 16 * ((p + ahead) // RING + 1))
                A(w_hi[:, s, :], raw[:, s, :], ACT.Copy).then_inc(hi_ready, 1)

            def copy_corr(half):
                A(corr[:, 2 * half:2 * half + 2, :], psum[:, 2 * half:2 * half + 2, T:2 * T], ACT.Copy)\
                    .then_inc(corr_out, 1)

            for q in range(KT // 2):
                act.wait_ge(x_turned, q + 1)
                A(x_t[:, 2 * q:2 * q + 2, 0:T], psum[:, q, :].rearrange("p (k t) -> p k t", k=2), ACT.Copy)\
                    .then_inc(x_hi_out, 1)
                if q % 2:
                    split(0, q // 2, 0)
            act.wait_ge(lam_pre, 1)
            A(lamt[:, 1, :], lamt[:, 0, :], ACT.Exp, scale=-1.0).then_inc(lam_exp, 1)
            act.wait_ge(lrw_landed, 16)
            act.wait_ge(lr_set, 2)
            A(lr_hi[:, :, 0:RANK], lr_raw[:, :, :], ACT.Copy).then_inc(lr_hi_ready, 1)
            act.wait_ge(mask_ready, 1)
            act.wait_ge(dve_pro, 2)
            with act.Fori(0, N_RX) as j:
                for p in range(SLOTS):
                    split(j + I_RX, p)
                    if p % 4 == 3:
                        half = p // 4
                        act.wait_ge(conv_lo, FREE + 2 * j + half)
                        A(rx_pad[:, half, :, CONV - 1:], psum[:, 2 * half:2 * half + 2, 0:T], ACT.Copy)\
                            .then_inc(group_read, 1)
                        act.wait_ge(group_read, 2 * j + half + 1)
                        for c in range(2):
                            t = 4 * j + 2 * half + c
                            r = A(conv_y[:, c, :], rx_pad[:, half, c, 0:T], ACT.Identity,
                                  bias=pcol("conv_b", t), scale=pcol("conv_w", t))
                            r.then_inc(tap0, 1)
                    if p in (5, 7):
                        half = p // 7
                        act.wait_ge(conv_out, 2 * j + half + 1)
                        A(b_t[:, bass.ds(4 * j + 2 * half, 2), 0:T], conv_y[:, :, :], ACT.Copy).then_inc(conv_hi, 1)

            act.wait_ge(lr_done, 1)
            A(lr_t[:, :], psum[0:RANK, 4, 0:T], ACT.Copy).then_inc(lr_ready, 1)
            for p in range(SLOTS):
                split(I_LG, p)
                for g, name in enumerate(("b_a", "b_x")):
                    for c in range(2):
                        t = 2 * p + c
                        r = A(gates[:, t, g * T:(g + 1) * T], psum[:, 4 * (p % 2) + 2 * g + c, 0:T], ACT.Sigmoid,
                              bias=pcol(name, t))
                r.then_inc(lg_read, 1)

            act.wait_ge(lru_c_ready, 1)
            with act.Fori(0, HEADS) as j:
                it = 4 * j + I_HEAD

                def decays(m):
                    if m == 0:
                        act.wait_ge(h_ready, FREE + j)
                        act.wait_ge(lg_read, SLOTS)
                    for f, to in ((ACT.Exp, lru_a), (ACT.Tanh, lru_m)):
                        for c in (2 * m, 2 * m + 1):
                            t = bass.ds(4 * j + c, 1)
                            A(to[:, c, :], gates[:, t, 0:T].rearrange("p a t -> p (a t)"), f, scale=lru_c[:, t])\
                                .then_inc(decay_exp, 1)

                for p in range(SLOTS):
                    split(it, p)
                    if p < 2:
                        decays(p)
                    if p == 4:
                        act.wait_ge(ms_done, FREE + j)
                        act.wait_ge(decay_exp, 8 * j + 8)
                        A(a_sq, lru_a[:, :, :], ACT.Square).then_inc(decay_sq, 1)
                    if p == 2:
                        act.wait_ge(alpha_out, j + 1)
                        A(e_neg[:, :, :], e_neg[:, :, :], ACT.Exp, scale=-1.0).then_inc(ls_exp, 1)
                    if p == 6:
                        act.wait_ge(ls_exp, j + 1)
                        A(e_neg[:, :, :], e_neg[:, :, :], ACT.Ln, bias=one_col[:, 0:1]).then_inc(ls_ln, 1)
                for p in range(SLOTS):
                    if p == 0:
                        act.wait_ge(bc_ready, j + 1)
                        A(e_pos[:, :, :], bc[:, :, :], ACT.Exp, scale=1.0 / TAU).then_inc(e_pos_ready, 1)
                        A(e_neg[:, :, :], bc[:, :, :], ACT.Exp, scale=-1.0 / TAU).then_inc(e_neg_ready, 1)
                    if p == 1:
                        act.wait_ge(k_diff, FREE + j + 1)
                        A(k_end[:, :, :], k_end[:, :, :], ACT.Exp, scale=-1.0 / TAU).then_inc(e_end_ready, 1)
                    if p == 3:
                        act.wait_ge(gap_ready, j + 1)
                        A(lru_m[:, :, :], lru_m[:, :, :], ACT.Sqrt, scale=-1.0).then_inc(gap_root, 1)
                    split(it + 1, p)
                    if p == 6:
                        act.wait_ge(kt_done, j + 1)
                        for at in (0, CHUNK):
                            own = slice(at, at + CHUNK)
                            r = A(scores[own, :, own], psum[own, 5, 0:T].rearrange("p (t i) -> p t i", t=TT)[:, :, own],
                                  ACT.Copy)
                        r.then_inc(sc_out, 1)
                        A(k_end_t[:, :, :], psum[:, 4, :].rearrange("p (t c) -> p t c", t=TT), ACT.Copy)\
                            .then_inc(kt_out, 1)
                    if p == 7:
                        A(v_h[:, :, :], psum[:, 6:8, :], ACT.Copy).then_inc(v_out, 1)
                for p in range(SLOTS):
                    split(it + 2, p)
                    if p % 4 == 3:
                        two = slice(2 * (p // 4), 2 * (p // 4) + 2)
                        if p == 3:
                            act.wait_ge(og_ready, FREE + 2 * j)
                        A(silu_g[:, two, :], psum[:, two, 0:T], ACT.Silu).then_inc(act_ready, 1)
                for p in range(SLOTS):
                    if p == 6:
                        act.wait_ge(og_ready, FREE + 2 * j + 2)
                    split(it + 3, p)
                    if p == 0:
                        act.wait_ge(chunk_done, 4 * j + 4)
                        act.wait_ge(h_ready, FREE + j + 1)
                        A(o_sq[:, :, :, :], psum[:, 4:6, :].rearrange("p t (b i) -> p t b i", b=4), ACT.Square)\
                            .then_inc(sq_ready, 1)
                    if p == 3:
                        act.wait_ge(rms_inv, j + 1)
                        A(rstd[:, :, :], rstd[:, :, :], ACT.Sqrt).then_inc(rms_root, 1)
                    if p == 6:
                        A(o_t[:, bass.ds(4 * j, 4), 0:T], o_g, ACT.Copy).then_inc(og_hi, 1)
                    if p % 4 == 3:
                        two = slice(2 * (p // 4), 2 * (p // 4) + 2)
                        if p == 3:
                            act.wait_ge(b_lo, FREE + 2 * j)
                        A(y_act[:, two, :], psum[:, two, 0:T], ACT.Gelu_apprx_tanh).then_inc(act_ready, 1)
                    if p in (4, 7):
                        half = p // 7
                        act.wait_ge(b_ready, FREE + 2 * j + half + 1)
                        A(b_t[:, bass.ds(4 * j + 2 * half, 2), 0:T], y_act[:, 2 * half:2 * half + 2, :], ACT.Copy)\
                            .then_inc(b_hi, 1)

            def stage_tile(m, source):
                A(stage[:, m, 0:T], source, ACT.Copy).then_inc(stage_hi, 1)

            act.wait_ge(b_lo, FREE + 2 * HEADS)
            A(scratch[:, 0:1], one_col[:, :], ACT.Sigmoid).then_inc(table_ready, 1)

            def merge_iteration(j, k, base, then_stage=False):
                for p in range(SLOTS):
                    split(j + base, p)
                    if p == 3:
                        copy_corr(0)
                        act.wait_ge(group_read, 2 * j + G_B + 2 * k * N_B + 1)
                        A(gsum[:, :, :], gsum[:, :, :], ACT.Sigmoid).then_inc(act_ready, 1)
                    if p == 5 and then_stage:
                        act.wait_ge(merged_ready, FREE + N_B + 2)
                        for m in range(4):
                            stage_tile(m, merged[:, m, :])
                    if p == 7:
                        copy_corr(1)

            with act.Fori(0, N_B) as j:
                merge_iteration(j, 0, I_B)
            with act.Fori(0, N_A - 1) as j:
                merge_iteration(j, 1, I_A)
            merge_iteration(N_A - 1, 1, I_A, then_stage=True)
            act.wait_ge(piece_done, SLOTS * I_OUT)
            act.dma_start(res[:, :, :], x.rearrange("(t p) d -> p t d", p=P)).then_inc(res_landed, 16)
            act.dma_start(tok_g1[:, :], ln1_g.to_broadcast([P, D])).then_inc(tok_landed, 16)
            act.dma_start(tok_b1[:, :], ln1_b.to_broadcast([P, D])).then_inc(tok_landed, 16)

            def token_major(it, j, source, last_it):
                ahead = SLOTS
                if last_it:
                    ahead = SLOTS - RING if source is h_ff else SLOTS - 3
                for p in range(ahead):
                    split(it, p)
                    if p % 2 == 1 and not last_it:
                        m = p // 2
                        act.wait_ge(piece_done, SLOTS * it + p + 1)
                        stage_tile(m, source[:, bass.ds(4 * j + 4 + m, 1), :].rearrange("p a t -> p (a t)"))

            A(scratch[:, 1:2], scratch[:, 0:1], ACT.Sqrt).then_inc(table_ready, 1)
            act.wait_ge(merged_ready, FREE + 2 * N_B)
            with act.Fori(0, N_OUT - 1) as j:
                token_major(j + I_OUT, j, merged, False)
            token_major(I_OUT + N_OUT - 1, 0, merged, True)

            def normalise(tt, ln):
                act.wait_ge(ln_inv, TT * ln + tt + 1)
                A(mv[:, tt, 2:3], mv[:, tt, 2:3], ACT.Sqrt).then_inc(ln_root, 1)
                act.wait_ge(ln_root, 2 * (TT * ln + tt) + 1)
                A(mv[:, tt, 3:4], mv[:, tt, 3:4], ACT.Copy, scale=mv[:, tt, 2:3]).then_inc(ln_root, 1)
                act.wait_ge(ln_root, 2 * (TT * ln + tt) + 2)
                for b in range(4):
                    z = res[:, tt, b * QUARTER:(b + 1) * QUARTER]
                    A(z, z, ACT.Identity, bias=mv[:, tt, 3:4], scale=mv[:, tt, 2:3]).then_inc(z_norm, 1)

            def ln_hi_part(tt, b):
                A(x_t[:, 4 * b:4 * b + 4, tt * P:(tt + 1) * P], ln_t[:, ln_place(tt, b), :, :], ACT.Copy)\
                    .then_inc(ln_hi[tt], 1)

            def tile0_channels(b):
                act.wait_ge(ln_turned[0], b + 1)
                for i in range(4):
                    r = A(ln_t[:, ln_place(0, b), i, :], psum[:, LN_BANK[0][b], i * P:(i + 1) * P], ACT.Identity,
                          bias=pcol("ln1_b", 4 * b + i), scale=pcol("ln1_g", 4 * b + i))
                r.then_inc(ln_out[0], 1)
                act.wait_ge(ln_out[0], b + 1)
                ln_hi_part(0, b)

            def tile1_hi(b):
                act.wait_ge(ln_out[1], b + 1)
                ln_hi_part(1, b)

            last = I_FFN - 1
            normalise(0, 0)
            split(last, SLOTS - 3)
            tile0_channels(0)
            normalise(1, 0)
            tile1_hi(0)
            tile0_channels(1)
            tile1_hi(1)
            split(last, SLOTS - 2)
            tile0_channels(2)
            tile1_hi(2)
            split(last, SLOTS - 1)
            tile0_channels(3)
            tile1_hi(3)

            A(scratch[:, 1:2], scratch[:, 0:1], ACT.Silu).then_inc(table_ready, 1)

            def ffn_iteration(j, then_stage=False):
                for p in range(SLOTS):
                    split(j + I_FFN, p)
                    if p == 3:
                        copy_corr(0)
                        act.wait_ge(group_read, 2 * j + G_FFN + 1)
                        act.wait_ge(ff_ready, FREE + j)
                        A(yb[:, :, :], gsum[:, :, :], ACT.Silu).then_inc(act_ready, 1)
                    if p == 5 and then_stage:
                        act.wait_ge(ff_ready, FREE + 2)
                        for m in range(4):
                            stage_tile(m, h_ff[:, m, :])
                    if p == 7:
                        copy_corr(1)

            with act.Fori(0, N_FFN - 1) as j:
                ffn_iteration(j)
            ffn_iteration(N_FFN - 1, then_stage=True)
            A(scratch[:, 1:2], scratch[:, 0:1], ACT.Sqrt).then_inc(table_ready, 1)
            act.wait_ge(ff_ready, FREE + N_FFN)
            with act.Fori(0, N_DOWN - 1) as j:
                token_major(j + I_DOWN, j, h_ff, False)
            token_major(I_DOWN + N_DOWN - 1, 0, h_ff, True)
            normalise(0, 1)
            act.wait_ge(ln_inv, 2 * TT)
            A(mv[:, 1, 2:3], mv[:, 1, 2:3], ACT.Sqrt).then_inc(ln_root, 1)

        @block.vector
        def _(dve):
            tt_op, ts_op, stt = nc.vector.tensor_tensor, nc.vector.tensor_scalar, nc.vector.scalar_tensor_tensor

            def split(it, p, ahead=RING):
                s = p % RING
                dve.wait_ge(hi_ready, SLOTS * it + p + ahead + 1)
                tt_op(w_lo[:, s, :], raw[:, s, :], w_hi[:, s, :].bitcast(F32), ALU.subtract).then_inc(lo_ready, 1)

            def group_sum(to, half, g):
                dve.wait_ge(corr_out, g - G_B + 1)
                tt_op(to, psum[:, 2 * half:2 * half + 2, 0:T], corr[:, 2 * half:2 * half + 2, :], ALU.add)\
                    .then_inc(group_read, 1)

            for free in (state_ready, dec_ready, k_diff, o_done, og_ready, h_ready, b_lo, conv_lo, merged_ready,
                         ff_ready, og_lo, b_ready):
                dve.sem_inc(free, FREE)
            pro = Steps(dve, dve_pro)
            pro.step(nc.vector.memset(rx_pad[:, :, :, 0:CONV - 1], 0.0))
            pro.step(nc.vector.memset(one_col[:, :], 1.0))
            for q in range(KT // 2):
                dve.wait_ge(x_hi_out, q + 1)
                tt_op(x_t[:, 2 * q:2 * q + 2, T:2 * T], psum[:, q, :].rearrange("p (k t) -> p k t", k=2),
                      x_t[:, 2 * q:2 * q + 2, 0:T].bitcast(F32), ALU.subtract).then_inc(x_lo_out, 1)
                if q % 2:
                    split(0, q // 2, 0)
            dve.wait_ge(par_landed, 16)
            lam = pcol("lambda", 0, KT)
            stt(lamt[:, 0, :], lam, -1.0, lam, ALU.mult, ALU.max).then_inc(lam_pre, 1)

            dve.wait_ge(lr_hi_ready, 1)
            tt_op(lr_lo[:, :, 0:RANK], lr_raw[:, :, :], lr_hi[:, :, 0:RANK].bitcast(F32), ALU.subtract)\
                .then_inc(lr_lo_ready, 1)
            per = 2 * 2 * (CONV - 2)
            with dve.Fori(0, N_RX) as j:
                own = Steps(dve, dve_rx, j, per)
                for p in range(SLOTS):
                    split(j + I_RX, p)
                    if p % 4 == 3:
                        half = p // 4
                        b = 2 * j + half
                        for k in range(1, CONV):
                            if k == 1:
                                dve.wait_ge(tap0, 2 * b + 2)
                            else:
                                own.wait()
                            for c in range(2):
                                w = par[:, bass.ds(4 * j + PAR["conv_w"] + k * KT + 2 * half + c, 1)]
                                r = stt(conv_y[:, c, :], rx_pad[:, half, c, k:k + T], w, conv_y[:, c, :],
                                        ALU.mult, ALU.add)
                                if k < CONV - 1:
                                    own.step(r)
                        r.then_inc(conv_out, 1)
                        dve.wait_ge(conv_hi, b + 1)
                        tile = bass.ds(4 * j + 2 * half, 2)
                        tt_op(b_t[:, tile, T:2 * T], conv_y[:, :, :], b_t[:, tile, 0:T].bitcast(F32), ALU.subtract)\
                            .then_inc(conv_lo, 1)
                own.end()

            y, s_, z_, acc = lamt[:, 1, :], lamt[:, 2, :], lamt[:, 3, :], lru_c[:, :]

            def log1p_start():
                dve.wait_ge(lam_exp, 1)
                pro.step(ts_op(s_, y, 2.0, None, ALU.add))
                pro.wait()
                pro.step(nc.vector.reciprocal(s_, s_))
                pro.wait()
                pro.step(tt_op(s_, s_, y, ALU.mult))
                pro.wait()
                pro.step(tt_op(z_, s_, s_, ALU.mult))
                pro.step(nc.vector.memset(acc, 1.0 / (2 * LOG1P_TERMS - 1)))

            def log1p_terms(first, end):
                for n in range(LOG1P_TERMS - 2 - first, LOG1P_TERMS - 2 - end, -1):
                    pro.wait()
                    pro.step(tt_op(acc, acc, z_, ALU.mult))
                    pro.wait()
                    pro.step(ts_op(acc, acc, 1.0 / (2 * n + 1), None, ALU.add))

            def lru_scale():
                pro.wait()
                pro.step(tt_op(acc, acc, s_, ALU.mult))
                pro.step(ts_op(y, lam, -1.0, 0.0, ALU.mult, ALU.max))
                pro.wait()
                pro.step(ts_op(y, y, -LRU_C, None, ALU.mult))
                pro.wait()
                stt(acc, acc, -2.0 * LRU_C, y, ALU.mult, ALU.add).then_inc(lru_c_ready, 1)

            for p in range(SLOTS):
                split(I_LG, p)
                if p == 1:
                    log1p_start()
                if 2 <= p <= 5:
                    log1p_terms(2 * (p - 2), 2 * (p - 1))
                if p == 6:
                    lru_scale()

            per = 2 + 1 + 1 + 1
            with dve.Fori(0, HEADS) as j:
                it = 4 * j + I_HEAD
                own = Steps(dve, dve_head, j, per)

                def lru_scan():
                    dve.wait_ge(gap_root, j + 1)
                    dve.wait_ge(b_ready, FREE + 2 * j)
                    dve.wait_ge(ix_ready, SLOTS)
                    own.step(tt_op(h_lru[:, :, :], gates[:, bass.ds(4 * j, 4), T:2 * T], lru_m[:, :, :], ALU.mult))
                    own.wait()
                    for c in range(4):
                        r = nc.vector.tensor_tensor_scan(h_lru[:, c, :], lru_a[:, c, :], h_lru[:, c, :], 0.0,
                                                         ALU.mult, ALU.add)
                    r.then_inc(h_ready, 1)

                for p in range(SLOTS):
                    split(it, p)
                    if p == 1:
                        dve.wait_ge(alpha_done, j + 1)
                        dve.wait_ge(state_ready, FREE + 3 * j)
                        dve.wait_ge(dec_ready, FREE + 3 * j)
                        for c in range(2):
                            own.step(ts_op(e_pos[:, c, :], psum[:, 4, c * T:(c + 1) * T], pcol("b_alpha", 2 * j + c),
                                           None, ALU.add))
                        own.wait()
                        stt(e_neg[:, :, :], e_pos[:, :, :], -1.0, e_pos[:, :, :], ALU.mult, ALU.max)\
                            .then_inc(alpha_out, 1)
                    if p == 5:
                        dve.wait_ge(decay_sq, j + 1)
                        stt(lru_m[:, :, :], a_sq, 1.0, lru_m[:, :, :], ALU.add, ALU.mult).then_inc(gap_ready, 1)
                    if p == 7:
                        dve.wait_ge(ls_ln, j + 1)
                        own.step(stt(e_pos[:, :, :], e_pos[:, :, :], 0.0, e_neg[:, :, :], ALU.min, ALU.subtract))
                        own.wait()
                        dve.wait_ge(mask_ready, 1)
                        dve.wait_ge(k_diff, FREE + j)
                        nc.vector.tensor_tensor_scan(bc[:, :, :].rearrange("p c t -> p (c t)"), chunk_mask[:, :],
                                                     e_pos[:, :, :].rearrange("p c t -> p (c t)"), 0.0,
                                                     ALU.mult, ALU.add).then_inc(bc_ready, 1)
                        dve.wait_ge(bc_ready, j + 1)
                        v = lambda t: t[:, :, :].rearrange("p c (n t) -> p (c n) t", t=CHUNK)
                        tt_op(v(k_end), v(bc), v(bc)[:, :, CHUNK - 1:CHUNK].to_broadcast([P, 2 * NCHUNK, CHUNK]),
                              ALU.subtract).then_inc(k_diff, 1)
                for p in range(SLOTS):
                    split(it + 1, p)
                    if p == 1:
                        dve.wait_ge(e_pos_ready, j + 1)
                        dve.wait_ge(piece_done, SLOTS * it + SLOTS)
                        dve.wait_ge(og_lo, FREE + j)
                        stt(qk_dec[:, 0, :, :], psum[:, 0:2, 0:T], DK ** -0.5, e_pos[:, :, :], ALU.mult, ALU.mult)\
                            .then_inc(dec_ready, 1)
                        dve.wait_ge(e_neg_ready, j + 1)
                        tt_op(qk_dec[:, 1, :, :], psum[:, 2:4, 0:T], e_neg[:, :, :], ALU.mult).then_inc(dec_ready, 1)
                    if p == 2:
                        dve.wait_ge(e_end_ready, j + 1)
                        tt_op(k_end[:, :, :], psum[:, 2:4, 0:T], k_end[:, :, :], ALU.mult).then_inc(dec_ready, 1)
                    if p == 4:
                        lru_scan()
                for p in range(SLOTS):
                    if p in (2, 4, 6):
                        n = p // 2 - 1
                        dve.wait_ge(chunk_done, 4 * j + n + 1)
                        dve.wait_ge(state_ready, FREE + 3 * j + n)
                        for c in range(2):
                            if n == 0:
                                r = nc.vector.tensor_copy(state[:, c, :], psum[:, 6 + c, :])
                            else:
                                at = n * CHUNK + CHUNK - 1
                                r = stt(state[:, c, :], state[:, c, :], e_pos[:, c, at:at + 1], psum[:, 6 + c, :],
                                        ALU.mult, ALU.add)
                        r.then_inc(state_ready, 1)
                    split(it + 2, p)
                for p in range(SLOTS):
                    split(it + 3, p)
                    if p == 2:
                        dve.wait_ge(ms_done, FREE + j + 1)
                        own.step(ts_op(rstd[:, :, :], psum[:, 6, 0:T].rearrange("p (t i) -> p t i", t=TT), EPS, None,
                                       ALU.add))
                        own.wait()
                        nc.vector.reciprocal(rstd[:, :, :], rstd[:, :, :]).then_inc(rms_inv, 1)
                    if p == 4:
                        dve.wait_ge(rms_root, j + 1)
                        for tt in range(TT):
                            r = tt_op(o_g[:, :, tt * P:(tt + 1) * P],
                                      psum[:, 4 + tt, :].rearrange("p (b i) -> p b i", b=4),
                                      rstd[:, tt:tt + 1, :].to_broadcast([P, 4, P]), ALU.mult)
                            r.then_inc(o_done, 1)
                        dve.wait_ge(o_done, FREE + 2 * j + 2)
                        dve.wait_ge(act_ready, ACT_FREE + 4 * j + 2)
                        for b in range(4):
                            r = stt(o_g[:, b, :], o_g[:, b, :], pcol("norm_g", b), silu_g[:, b, :], ALU.mult, ALU.mult)
                            if b % 2:
                                r.then_inc(og_ready, 1)
                    if p % 4 == 3:
                        half = p // 4
                        y = y_act[:, 2 * half:2 * half + 2, :]
                        dve.wait_ge(act_ready, ACT_FREE + 4 * j + 3 + half)
                        dve.wait_ge(h_ready, FREE + j + 1)
                        tt_op(y, y, h_lru[:, 2 * half:2 * half + 2, :], ALU.mult).then_inc(b_ready, 1)
                        dve.wait_ge(b_hi, 2 * j + half + 1)
                        tile = bass.ds(4 * j + 2 * half, 2)
                        tt_op(b_t[:, tile, T:2 * T], y, b_t[:, tile, 0:T].bitcast(F32), ALU.subtract)\
                            .then_inc(b_lo, 1)
                    if p == 7:
                        dve.wait_ge(og_hi, j + 1)
                        tile = bass.ds(4 * j, 4)
                        tt_op(o_t[:, tile, T:2 * T], o_g, o_t[:, tile, 0:T].bitcast(F32), ALU.subtract)\
                            .then_inc(og_lo, 1)
                own.end()

            def stage_tile(n, m, source):
                dve.wait_ge(stage_hi, n + 1)
                tt_op(stage[:, m, T:2 * T], source, stage[:, m, 0:T].bitcast(F32), ALU.subtract)\
                    .then_inc(stage_ready, 1)

            def merge_iteration(j, k, base, then_stage=False):
                gb = G_B + 2 * k * N_B
                for p in range(SLOTS):
                    split(j + base, p)
                    if p == 3:
                        dve.wait_ge(merged_ready, FREE + j + k * N_B)
                        group_sum(gsum[:, :, :], 0, 2 * j + gb)
                    if p == 5 and then_stage:
                        for m in range(4):
                            stage_tile(m, m, merged[:, m, :])
                    if p == 7:
                        group_sum(yb[:, :, :], 1, 2 * j + gb + 1)
                        dve.wait_ge(group_read, 2 * j + gb + 2)
                        dve.wait_ge(act_ready, ACT_FREE + j + 4 * HEADS + k * N_B + 1)
                        to = merged[:, bass.ds(2 * j, 2), :]
                        if k == 0:
                            tt_op(to, gsum[:, :, :], yb[:, :, :], ALU.mult).then_inc(merged_ready, 1)
                        else:
                            tt_op(yb[:, :, :], gsum[:, :, :], yb[:, :, :], ALU.mult).then_inc(gated, 1)
                            dve.wait_ge(gated, j + 1)
                            tt_op(to, to, yb[:, :, :], ALU.add).then_inc(merged_ready, 1)

            with dve.Fori(0, N_B) as j:
                merge_iteration(j, 0, I_B)
            with dve.Fori(0, N_A - 1) as j:
                merge_iteration(j, 1, I_A)
            merge_iteration(N_A - 1, 1, I_A, then_stage=True)

            def token_major(it, j, first_tile, source, last_it=False):
                for p in range(SLOTS - RING if last_it else SLOTS):
                    split(it, p)
                    if p % 2 == 1 and not last_it:
                        m = p // 2
                        stage_tile(4 * j + 4 + m + first_tile, m,
                                   source[:, bass.ds(4 * j + 4 + m, 1), :].rearrange("p a t -> p (a t)"))

            def norm_stats(n, tt, end):
                own = Steps(dve, dve_ln)
                own.n = n
                summed = []

                def add_residual(b):
                    if tt == 0:
                        dve.wait_ge(tile0_done, (0 if end == I_FFN else 2) + b // 2 + 1)
                    elif b < 2:
                        dve.wait_ge(tile1_half, 1 if end == I_FFN else 2)
                    else:
                        dve.wait_ge(piece_done, SLOTS * end)
                    z, product = res[:, tt, b * QUARTER:(b + 1) * QUARTER], psum[:, 4 * tt + b, :]
                    if end == I_FFN:
                        own.step(stt(z, z, ALPHA, product, ALU.mult, ALU.add))
                    else:
                        own.step(tt_op(z, z, product, ALU.add))
                    summed.append(own.n)

                add_residual(0)
                for b in range(4):
                    if b < 3:
                        add_residual(b + 1)
                    dve.wait_ge(dve_ln, summed[b])
                    own.step(nc.vector.bn_stats(stats[:, tt, b, :], res[:, tt, b * QUARTER:(b + 1) * QUARTER]))
                own.wait()
                own.step(nc.vector.bn_aggr(mv[:, tt, 0:2], stats[:, tt, :, :].rearrange("p b s -> p (b s)")))
                own.wait()
                own.step(ts_op(mv[:, tt, 2:3], mv[:, tt, 1:2], EPS, None, ALU.add))
                own.step(ts_op(mv[:, tt, 3:4], mv[:, tt, 0:1], -1.0, None, ALU.mult))
                own.wait()
                nc.vector.reciprocal(mv[:, tt, 2:3], mv[:, tt, 2:3]).then_inc(ln_inv, 1)
                return own.n

            dve.wait_ge(merged_ready, FREE + 2 * N_B)
            with dve.Fori(0, N_OUT - 1) as j:
                token_major(j + I_OUT, j, 0, merged)
            token_major(I_OUT + N_OUT - 1, 0, 0, merged, last_it=True)

            dve.wait_ge(res_landed, 16)
            n_ln = norm_stats(0, 0, I_FFN)
            assert n_ln == LN_STEPS
            n_ln = norm_stats(n_ln, 1, I_FFN)

            def ln_lo_part(tt, b):
                dve.wait_ge(ln_hi[tt], b + 1)
                tt_op(x_t[:, 4 * b:4 * b + 4, T + tt * P:T + (tt + 1) * P], ln_t[:, ln_place(tt, b), :, :],
                      x_t[:, 4 * b:4 * b + 4, tt * P:(tt + 1) * P].bitcast(F32), ALU.subtract).then_inc(ln_lo[tt], 1)

            def tile1_channels(b):
                dve.wait_ge(ln_turned[1], b + 1)
                if b >= 2:
                    dve.wait_ge(ln_lo[0], b - 1)
                for i in range(4):
                    r = ts_op(ln_t[:, ln_place(1, b), i, :], psum[:, LN_BANK[1][b], i * P:(i + 1) * P],
                              pcol("ln1_g", 4 * b + i), pcol("ln1_b", 4 * b + i), ALU.mult, ALU.add)
                r.then_inc(ln_out[1], 1)

            split(I_FFN - 1, SLOTS - RING)
            ln_lo_part(0, 0)
            tile1_channels(0)
            for b in range(4):
                if b < 3:
                    tile1_channels(b + 1)
                ln_lo_part(1, b)
                if b < 3:
                    split(I_FFN - 1, SLOTS - RING + b + 1)
                    ln_lo_part(0, b + 1)

            def ffn_iteration(j, then_stage=False):
                for p in range(SLOTS):
                    split(j + I_FFN, p)
                    if p == 3:
                        dve.wait_ge(ff_ready, FREE + j)
                        group_sum(gsum[:, :, :], 0, 2 * j + G_FFN)
                    if p == 5 and then_stage:
                        for m in range(4):
                            stage_tile(4 * N_OUT + m, m, h_ff[:, m, :])
                    if p == 7:
                        dve.wait_ge(act_ready, ACT_FREE + j + 4 * HEADS + 2 * N_B + 1)
                        group_sum(gsum[:, :, :], 1, 2 * j + G_FFN + 1)
                        dve.wait_ge(group_read, 2 * j + G_FFN + 2)
                        tt_op(h_ff[:, bass.ds(2 * j, 2), :], gsum[:, :, :], yb[:, :, :], ALU.mult)\
                            .then_inc(ff_ready, 1)

            with dve.Fori(0, N_FFN - 1) as j:
                ffn_iteration(j)
            ffn_iteration(N_FFN - 1, then_stage=True)
            dve.wait_ge(ff_ready, FREE + N_FFN)
            with dve.Fori(0, N_DOWN - 1) as j:
                token_major(j + I_DOWN, j, 4 * N_OUT, h_ff)
            token_major(I_DOWN + N_DOWN - 1, 0, 0, h_ff, last_it=True)

            dve.wait_ge(pool_res, TT)
            dve.wait_ge(z_norm, 4 * TT)
            n_ln = norm_stats(n_ln, 0, ITERS)
            n_ln = norm_stats(n_ln, 1, ITERS)
            dve.wait_ge(dve_ln, n_ln)
            dve.wait_ge(ln2_landed, 32)
            for b in range(5):
                if b < 4:
                    part = slice(b * QUARTER, (b + 1) * QUARTER)
                    o = res[:, 1, part]
                    stt(o, o, mv[:, 1, 3:4], tok_g1[:, part], ALU.add, ALU.mult).then_inc(scaled, 1)
                if b > 0:
                    part = slice((b - 1) * QUARTER, b * QUARTER)
                    o = res[:, 1, part]
                    dve.wait_ge(scaled, b)
                    dve.wait_ge(ln_root, 2 * (2 * TT - 1) + 1)
                    stt(o, o, mv[:, 1, 2:3], tok_b1[:, part], ALU.mult, ALU.add).then_inc(out_ready, 1)

        @block.gpsimd
        def _(pool):
            pool.memset(ident[:, :], 0.0).then_inc(pool_set, 1)
            pool.wait_ge(pool_set, 1)
            pool.affine_select(out=ident[:, :], in_=ident[:, :], compare_op=ALU.not_equal, fill=1.0, base=0,
                               pattern=[[-1, P]], channel_multiplier=1).then_inc(consts, 1)
            pool.memset(ones_dv[:, :], 1.0 / DV).then_inc(consts, 1)
            pool.memset(chunk_mask[:, :], 1.0).then_inc(pool_set, 1)
            pool.memset(scores[:, :, :], 0.0).then_inc(pool_set, 1)
            for t in (lr_hi, lr_lo):
                pool.memset(t[:, :, RANK:P].bitcast(F32), 0.0).then_inc(lr_set, 1)
            pool.wait_ge(pool_set, 3)
            pool.memset(chunk_mask[:, :].rearrange("p (n t) -> p n t", t=CHUNK)[:, :, 0:1], 0.0).then_inc(mask_ready, 1)
            pool.dma_start(alpha_cur[:, :], w_alpha[:, 0:DK]).then_inc(alpha_landed, 16)
            for p in range(SLOTS):
                two, part = slice(2 * p, 2 * p + 2), slice(2 * (p % 2), 2 * (p % 2) + 2)
                pool.wait_ge(conv_lo, FREE + p + 1)
                if p > 0:
                    pool.wait_ge(ix_ready, p)
                pool.tensor_tensor(h_lru[:, part, :], b_t[:, two, 0:T].bitcast(F32), b_t[:, two, T:2 * T].bitcast(F32),
                                   ALU.add).then_inc(x_conv, 1)
                pool.wait_ge(x_conv, p + 1)
                pool.wait_ge(lg_read, p + 1)
                pool.tensor_tensor(gates[:, two, T:2 * T], gates[:, two, T:2 * T], h_lru[:, part, :], ALU.mult)\
                    .then_inc(ix_ready, 1)
            pool.wait_ge(ix_ready, SLOTS)
            for j in range(HEADS):
                if j + 1 < HEADS:
                    pool.wait_ge(alpha_done, j + 1)
                    pool.dma_start(alpha_cur[:, :], w_alpha[:, DK * (j + 1):DK * (j + 2)]).then_inc(alpha_landed, 16)
                pool.wait_ge(sc_out, j + 1)
                pool.affine_select(out=scores[:, :, :], in_=scores[:, :, :], compare_op=ALU.is_ge, fill=0.0, base=0,
                                   pattern=[[0, TT], [1, P]], channel_multiplier=-1).then_inc(sc_masked, 1)
                pool.wait_ge(sq_ready, j + 1)
                pool.tensor_tensor(o_sq[:, :, 0:2, :], o_sq[:, :, 0:2, :], o_sq[:, :, 2:4, :], ALU.add)\
                    .then_inc(sq_step, 1)
                pool.wait_ge(sq_step, j + 1)
                pool.tensor_tensor(o_sq[:, :, 0, :], o_sq[:, :, 0, :], o_sq[:, :, 1, :], ALU.add).then_inc(sq_sum, 1)
                pool.wait_ge(sq_sum, j + 1)
            pool.wait_ge(tok_landed, 32)
            for tt in range(TT):
                pool.wait_ge(ln_turned[tt], 4)
                z = res[:, tt, :]
                pool.tensor_tensor(z, z, tok_g1[:, :], ALU.mult).then_inc(res_step, 1)
                pool.wait_ge(res_step, 2 * tt + 1)
                pool.tensor_tensor(z, z, tok_b1[:, :], ALU.add).then_inc(res_step, 1)
                pool.wait_ge(res_step, 2 * tt + 2)
                pool.tensor_scalar(z, z, ALPHA, None, ALU.mult).then_inc(pool_res, 1)
            pool.wait_ge(ln2_landed, 32)
            for b in range(4):
                part = slice(b * QUARTER, (b + 1) * QUARTER)
                pool.wait_ge(z_norm, 4 * TT + b + 1)
                o = res[:, 0, part]
                pool.tensor_tensor(o, o, tok_g1[:, part], ALU.mult).then_inc(res_step, 1)
                pool.wait_ge(res_step, 2 * TT + b + 1)
                pool.tensor_tensor(o, o, tok_b1[:, part], ALU.add).then_inc(out_ready_pool, 1)


def kernel(x, w_in, gla_w_alpha, gla_b_alpha, gla_norm_g, gla_w_o, conv_w, conv_b, lru_w_a, lru_b_a, lru_w_x, lru_b_x,
           lru_lambda, rnn_w_o, w_out, ln1_g, ln1_b, w_gate_up, w_down, ln2_g, ln2_b):
    import concourse.bacc as bacc
    from concourse.bass_utils import run_bass_kernel_spmd

    def tiles(a):
        return np.asarray(a).reshape(-1, P).T

    params = np.concatenate([tiles(a) for a in (conv_w, conv_b, lru_b_a, lru_b_x, lru_lambda, gla_b_alpha,
                                                gla_norm_g, ln1_g, ln1_b)], axis=1)
    lru_w = np.stack([np.asarray(a)[0].reshape(8, 2, P, DK) for a in (lru_w_a, lru_w_x)], axis=3)
    lru_w = lru_w.transpose(0, 2, 1, 3, 4).reshape(8, P, PIECE)
    arrays = {
        "x": np.asarray(x)[0], "w_in": np.asarray(w_in)[0], "w_alpha": np.asarray(gla_w_alpha)[0],
        "w_o": np.asarray(gla_w_o)[0], "lru_w": lru_w, "rnn_o": np.asarray(rnn_w_o)[0],
        "w_out": np.asarray(w_out)[0], "w_gu": np.asarray(w_gate_up)[0], "w_down": np.asarray(w_down)[0],
        "params": params, "ln1_g": np.asarray(ln1_g), "ln1_b": np.asarray(ln1_b),
        "ln2_g": np.asarray(ln2_g), "ln2_b": np.asarray(ln2_b),
    }
    nc = bacc.Bacc("TRN2", target_bir_lowering=False, num_devices=1)
    arrays = {k: np.ascontiguousarray(a) for k, a in arrays.items()}
    aps = {k: nc.dram_tensor(k, a.shape, mybir.dt.from_np(a.dtype), kind="ExternalInput").ap()
           for k, a in arrays.items()}
    out = nc.dram_tensor("out", (T, D), F32, kind="ExternalOutput").ap()
    build(nc, out=out, **aps)
    r = run_bass_kernel_spmd(nc, [arrays], core_ids=[0])
    return r.results[0]["out"].reshape(1, T, D)
```
